# Optimizing a Trainium2 kernel written in Bass

```python
import jax, jax.numpy as jnp
from jax import lax
import numpy as np
import jax
import jax.numpy as jnp

D_MODEL = 1024
BATCH = 1
SEQ = 512
DEPTH = 2

HEAD_DIM = 64
MIX_WIDTH = D_MODEL
ATT_Q_HEADS = (MIX_WIDTH // 2) // HEAD_DIM
ATT_KV_HEADS = 2
ATT_GROUP = ATT_Q_HEADS // ATT_KV_HEADS
ATT_WIDTH = ATT_Q_HEADS * HEAD_DIM
ATT_KV_WIDTH = ATT_KV_HEADS * HEAD_DIM
WINDOW = 128
BLOCK = 128
RWKV_HEADS = (MIX_WIDTH // 4) // HEAD_DIM
RWKV_WIDTH = RWKV_HEADS * HEAD_DIM
DECAY_LORA = 64
ICLR_LORA = 64
GATE_LORA = 128
RWKV_GN_EPS = 64e-5
CONV_WIDTH = MIX_WIDTH - ATT_WIDTH - RWKV_WIDTH
CONV_K = 3
ATT_PROJ_WIDTH = ATT_WIDTH + 2 * ATT_KV_WIDTH
RWKV_SIZES = (RWKV_WIDTH, RWKV_WIDTH, RWKV_WIDTH, DECAY_LORA, ICLR_LORA, GATE_LORA)
RWKV_PROJ_WIDTH = 3 * RWKV_WIDTH + DECAY_LORA + ICLR_LORA + GATE_LORA
CONV_PROJ_WIDTH = 3 * CONV_WIDTH
PROJ_WIDTH = ATT_PROJ_WIDTH + RWKV_PROJ_WIDTH + CONV_PROJ_WIDTH
D_FF = 2816
N_MOD = 9
EPS = 1e-6


def rms_norm(x, gain):
    xf = x.astype(jnp.float32)
    y = xf * lax.rsqrt(jnp.mean(xf * xf, axis=-1, keepdims=True) + EPS)
    return (y * gain.astype(jnp.float32)).astype(x.dtype)

def swiglu(x, w_in, w_out):
    gate, up = jnp.split(x @ w_in, 2, axis=-1)
    return (jax.nn.silu(gate) * up) @ w_out

def token_shift(p):
    return jnp.pad(p, ((0, 0), (1, 0), (0, 0)))[:, :-1]

def sliding_window_sink_attention(qkv, q_gain, k_gain, sinks):
    B, T, _ = qkv.shape
    nb = T // BLOCK
    q, k, v = jnp.split(qkv, [ATT_WIDTH, ATT_WIDTH + ATT_KV_WIDTH], axis=-1)
    q = rms_norm(q.reshape(B, T, ATT_Q_HEADS, HEAD_DIM), q_gain)
    k = rms_norm(k.reshape(B, T, ATT_KV_HEADS, HEAD_DIM), k_gain)
    v = v.reshape(B, T, ATT_KV_HEADS, HEAD_DIM)
    qb = q.reshape(B, nb, BLOCK, ATT_KV_HEADS, ATT_GROUP, HEAD_DIM)

    def band(z):
        zb = z.reshape(B, nb, BLOCK, ATT_KV_HEADS, HEAD_DIM)
        prev = jnp.pad(zb, ((0, 0), (1, 0), (0, 0), (0, 0), (0, 0)))[:, :-1]
        return jnp.concatenate([prev, zb], axis=2)

    kb, vb = band(k), band(v)
    scores = jnp.einsum('bnqhgd,bnkhd->bnhgqk', qb, kb).astype(jnp.float32) * (HEAD_DIM ** -0.5)
    blk = jnp.arange(nb)[:, None, None] * BLOCK
    q_pos = blk + jnp.arange(BLOCK)[None, :, None]
    k_pos = blk - BLOCK + jnp.arange(2 * BLOCK)[None, None, :]
    diff = q_pos - k_pos
    mask = (k_pos >= 0) & (diff >= 0) & (diff < WINDOW)
    scores = jnp.where(mask[None, :, None, None], scores, -jnp.inf)
    sink = sinks.astype(jnp.float32).reshape(ATT_KV_HEADS, ATT_GROUP)[None, None, :, :, None, None]
    sink = jnp.broadcast_to(sink, scores.shape[:-1] + (1,))
    probs = jax.nn.softmax(jnp.concatenate([scores, sink], axis=-1), axis=-1)[..., :-1]
    out = jnp.einsum('bnhgqk,bnkhd->bnqhgd', probs.astype(v.dtype), vb)
    return out.reshape(B, T, ATT_WIDTH)

def rwkv7_time_mix(p, mu, w0, w_w2, a0, w_a2, w_g2, k_k, k_a, r_k, gn_w, gn_b):
    B, T, _ = p.shape
    f32 = jnp.float32
    p = p + mu * (token_shift(p) - p)
    r, k, v, wd, ad, gd = jnp.split(p, np.cumsum(RWKV_SIZES)[:-1].tolist(), axis=-1)
    r, k, v = r.astype(f32), k.astype(f32), v.astype(f32)
    w_log = -jax.nn.softplus(-(w0 + jnp.tanh(wd) @ w_w2).astype(f32)) - 0.5
    decay = jnp.exp(-jnp.exp(w_log))
    a = jax.nn.sigmoid((a0 + ad @ w_a2).astype(f32))
    g = (jax.nn.sigmoid(gd) @ w_g2).astype(f32)
    kk = (k * k_k).reshape(B, T, RWKV_HEADS, HEAD_DIM)
    kk = kk / jnp.maximum(jnp.linalg.norm(kk, axis=-1, keepdims=True), 1e-12)
    k = k * (1.0 + (a - 1.0) * k_a)
    hs = lambda z: z.reshape(B, T, RWKV_HEADS, HEAD_DIM)
    r, k, v, a, decay = hs(r), hs(k), hs(v), hs(a), hs(decay)

    def step(S, inp):
        r_t, w_t, k_t, v_t, kk_t, a_t = inp
        s_kk = jnp.einsum('bhvk,bhk->bhv', S, kk_t)
        S = (S * w_t[:, :, None, :] - s_kk[..., None] * (kk_t * a_t)[:, :, None, :]
             + v_t[..., None] * k_t[:, :, None, :])
        return S, jnp.einsum('bhvk,bhk->bhv', S, r_t)

    xs = tuple(jnp.swapaxes(z, 0, 1) for z in (r, decay, k, v, kk, a))
    S0 = jnp.zeros((B, RWKV_HEADS, HEAD_DIM, HEAD_DIM), f32)
    _, y = lax.scan(step, S0, xs)
    y = jnp.swapaxes(y, 0, 1)
    mean = jnp.mean(y, axis=-1, keepdims=True)
    var = jnp.mean(jnp.square(y - mean), axis=-1, keepdims=True)
    y = ((y - mean) * lax.rsqrt(var + RWKV_GN_EPS)).reshape(B, T, RWKV_WIDTH) * gn_w + gn_b
    bonus = jnp.sum(r * k * r_k, axis=-1, keepdims=True) * v
    y = (y + bonus.reshape(B, T, RWKV_WIDTH)) * g
    return y.astype(p.dtype)

def short_conv_mix(p, conv_w):
    b_gate, c_gate, h = jnp.split(p, [CONV_WIDTH, 2 * CONV_WIDTH], axis=-1)
    u = c_gate * h
    y = lax.conv_general_dilated(u, conv_w[:, None, :].astype(u.dtype), window_strides=(1,),
                                 padding=[(CONV_K - 1, 0)], dimension_numbers=('NWC', 'WIO', 'NWC'),
                                 feature_group_count=CONV_WIDTH)
    return b_gate * y

def first_inputs(seed: int = 0) -> dict:
    key = jax.random.key(seed)
    ks = iter(jax.random.split(key, 32))
    nrm = lambda shape, s: jax.random.normal(next(ks), shape, jnp.float32) * s
    L, D = DEPTH, D_MODEL
    return {
        'x': nrm((BATCH, SEQ, D), 1.0),
        'c': nrm((BATCH, D), 1.0),
        'w_ada': nrm((L, D, N_MOD * D), 0.1 * D ** -0.5),
        'b_ada': nrm((L, N_MOD * D), 0.01),
        'g_ffn1': 1.0 + nrm((L, D), 0.05),
        'w_ffn1_in': nrm((L, D, 2 * D_FF), D ** -0.5),
        'w_ffn1_out': nrm((L, D_FF, D), D_FF ** -0.5),
        'g_mix': 1.0 + nrm((L, D), 0.05),
        'w_mix_in': nrm((L, D, PROJ_WIDTH), D ** -0.5),
        'w_mix_out': nrm((L, MIX_WIDTH, D), MIX_WIDTH ** -0.5),
        'att_q_gain': 1.0 + nrm((L, HEAD_DIM), 0.05),
        'att_k_gain': 1.0 + nrm((L, HEAD_DIM), 0.05),
        'att_sinks': nrm((L, ATT_Q_HEADS), 1.0),
        'rwkv_mu': jax.random.uniform(next(ks), (L, RWKV_PROJ_WIDTH), jnp.float32),
        'rwkv_w0': jax.random.uniform(next(ks), (L, RWKV_WIDTH), jnp.float32, -6.0, -1.0),
        'rwkv_w_w2': nrm((L, DECAY_LORA, RWKV_WIDTH), 0.1 * DECAY_LORA ** -0.5),
        'rwkv_a0': nrm((L, RWKV_WIDTH), 0.1),
        'rwkv_a_w2': nrm((L, ICLR_LORA, RWKV_WIDTH), 0.1 * ICLR_LORA ** -0.5),
        'rwkv_g_w2': nrm((L, GATE_LORA, RWKV_WIDTH), GATE_LORA ** -0.5),
        'rwkv_k_k': 1.0 + nrm((L, RWKV_WIDTH), 0.1),
        'rwkv_k_a': 1.0 + nrm((L, RWKV_WIDTH), 0.1),
        'rwkv_r_k': nrm((L, RWKV_HEADS, HEAD_DIM), 0.1),
        'rwkv_gn_w': 1.0 + nrm((L, RWKV_WIDTH), 0.05),
        'rwkv_gn_b': nrm((L, RWKV_WIDTH), 0.01),
        'conv_w': nrm((L, CONV_K, CONV_WIDTH), CONV_K ** -0.5),
        'g_ffn2': 1.0 + nrm((L, D), 0.05),
        'w_ffn2_in': nrm((L, D, 2 * D_FF), D ** -0.5),
        'w_ffn2_out': nrm((L, D_FF, D), D_FF ** -0.5),
    }

def first_block(x, c, w_ada, b_ada, g_ffn1, w_ffn1_in, w_ffn1_out, g_mix, w_mix_in, w_mix_out,
              att_q_gain, att_k_gain, att_sinks, rwkv_mu, rwkv_w0, rwkv_w_w2, rwkv_a0, rwkv_a_w2,
              rwkv_g_w2, rwkv_k_k, rwkv_k_a, rwkv_r_k, rwkv_gn_w, rwkv_gn_b, conv_w,
              g_ffn2, w_ffn2_in, w_ffn2_out):
    h = x
    B = x.shape[0]
    c_act = jax.nn.silu(c)
    for l in range(DEPTH):
        mod = (c_act @ w_ada[l] + b_ada[l]).reshape(B, N_MOD, D_MODEL)
        sh1, sc1, gt1, sh2, sc2, gt2, sh3, sc3, gt3 = [mod[:, i, None, :] for i in range(N_MOD)]
        hn = rms_norm(h, g_ffn1[l]) * (1.0 + sc1) + sh1
        h = h + 0.5 * (1.0 + gt1) * swiglu(hn, w_ffn1_in[l], w_ffn1_out[l])
        hn = rms_norm(h, g_mix[l]) * (1.0 + sc2) + sh2
        proj = hn @ w_mix_in[l]
        p_att, p_rwkv, p_conv = jnp.split(proj, [ATT_PROJ_WIDTH, ATT_PROJ_WIDTH + RWKV_PROJ_WIDTH], axis=-1)
        y_att = sliding_window_sink_attention(p_att, att_q_gain[l], att_k_gain[l], att_sinks[l])
        y_rwkv = rwkv7_time_mix(p_rwkv, rwkv_mu[l], rwkv_w0[l], rwkv_w_w2[l], rwkv_a0[l], rwkv_a_w2[l],
                                rwkv_g_w2[l], rwkv_k_k[l], rwkv_k_a[l], rwkv_r_k[l], rwkv_gn_w[l], rwkv_gn_b[l])
        y_conv = short_conv_mix(p_conv, conv_w[l])
        mixed = jnp.concatenate([y_att, y_rwkv, y_conv], axis=-1) @ w_mix_out[l]
        h = h + (1.0 + gt2) * mixed
        hn = rms_norm(h, g_ffn2[l]) * (1.0 + sc3) + sh3
        h = h + 0.5 * (1.0 + gt3) * swiglu(hn, w_ffn2_in[l], w_ffn2_out[l])
    return h


DEPTH_2 = 1

DSA_PATTERNS = ((128, 1), (512, 4), (2048, 16))
DSA_GROUPS = 3
DSA_HEADS = 8
DSA_HEAD_DIM = 64
DSA_WIDTH = DSA_HEADS * DSA_HEAD_DIM
DSA_BLOCK = 128
ROPE_THETA = 10000.0

GDN_HEADS = 8
GDN_KEY_DIM = 64
GDN_VAL_DIM = 64
GDN_K_WIDTH = GDN_HEADS * GDN_KEY_DIM
GDN_V_WIDTH = GDN_HEADS * GDN_VAL_DIM
GDN_CONV = 4
GDN_CHUNK = 64

NORM_EPS = 1e-6

IN_SIZES = (
    DSA_GROUPS * 3 * DSA_WIDTH,
    DSA_WIDTH,
    2 * GDN_K_WIDTH + GDN_V_WIDTH,
    GDN_V_WIDTH,
    GDN_HEADS,
    GDN_HEADS,
    D_MODEL,
    D_MODEL,
)
IN_WIDTH = sum(IN_SIZES)


def _rmsnorm(x, w):
    xf = x.astype(jnp.float32)
    y = xf * lax.rsqrt(jnp.mean(xf * xf, axis=-1, keepdims=True) + NORM_EPS)
    return (y * w.astype(jnp.float32)).astype(x.dtype)

def _l2norm(t):
    return t * lax.rsqrt(jnp.sum(t * t, axis=-1, keepdims=True) + NORM_EPS)

def _split_columns(h):
    parts, start = [], 0
    for size in IN_SIZES:
        parts.append(h[..., start:start + size])
        start += size
    return parts

def _rope_tables(seq, dim):
    inv_freq = ROPE_THETA ** (-jnp.arange(0, dim, 2, dtype=jnp.float32) / dim)
    ang = jnp.arange(seq, dtype=jnp.float32)[:, None] * inv_freq[None, :]
    ang = jnp.concatenate([ang, ang], axis=-1)
    return jnp.cos(ang), jnp.sin(ang)

def _apply_rope(t, cos, sin):
    half = t.shape[-1] // 2
    rot = jnp.concatenate([-t[..., half:], t[..., :half]], axis=-1)
    return t * cos[:, None, None, :] + rot * sin[:, None, None, :]

def _dilated_window_attention(q, k, v, window, dilation):
    b, s, h, dh = q.shape
    n_back = window // dilation
    sub_len = s // dilation
    n_blk = -(-sub_len // DSA_BLOCK)
    pad = n_blk * DSA_BLOCK - sub_len

    def to_blocks(t):
        t = t.reshape(b, sub_len, dilation, h, dh).transpose(0, 2, 1, 3, 4)
        t = jnp.pad(t, ((0, 0), (0, 0), (0, pad), (0, 0), (0, 0)))
        return t.reshape(b, dilation, n_blk, DSA_BLOCK, h, dh)

    def with_previous_block(t):
        prev = jnp.pad(t, ((0, 0), (0, 0), (1, 0), (0, 0), (0, 0), (0, 0)))[:, :, :-1]
        return jnp.concatenate([prev, t], axis=3)

    qb = to_blocks(q)
    kb = with_previous_block(to_blocks(k))
    vb = with_previous_block(to_blocks(v))
    scores = jnp.einsum('brnqhd,brnkhd->brnhqk', qb, kb) * (dh ** -0.5)
    qi = jnp.arange(DSA_BLOCK)[:, None]
    kj = jnp.arange(2 * DSA_BLOCK)[None, :]
    dist = qi + DSA_BLOCK - kj
    key_idx = jnp.arange(n_blk)[:, None, None] * DSA_BLOCK + kj - DSA_BLOCK
    valid = (dist >= 0) & (dist <= n_back) & (key_idx >= 0)
    scores = jnp.where(valid[:, None], scores, -jnp.inf)
    m = jnp.max(scores, axis=-1, keepdims=True)
    p = jnp.exp(scores - m)
    den = jnp.sum(p, axis=-1, keepdims=True)
    o = jnp.einsum('brnhqk,brnkhd->brnqhd', p / den, vb)
    lse = (m + jnp.log(den))[..., 0].transpose(0, 1, 2, 4, 3)

    def from_blocks(t):
        t = t.reshape(b, dilation, n_blk * DSA_BLOCK, *t.shape[4:])[:, :, :sub_len]
        t = jnp.moveaxis(t, 1, 2)
        return t.reshape(b, s, *t.shape[3:])

    return from_blocks(o), from_blocks(lse)

def _dilated_mixture(q, k, v):
    outs, lses = [], []
    for g, (window, dilation) in enumerate(DSA_PATTERNS):
        o, lse = _dilated_window_attention(q[:, :, g], k[:, :, g], v[:, :, g], window, dilation)
        outs.append(o)
        lses.append(lse)
    wts = jax.nn.softmax(jnp.stack(lses), axis=0)
    o = jnp.einsum('gbsh,gbshd->bshd', wts, jnp.stack(outs))
    return o.reshape(o.shape[0], o.shape[1], -1)

def _causal_depthwise_conv(x, w):
    k, c = w.shape
    return lax.conv_general_dilated(
        x, w[:, None, :].astype(x.dtype), window_strides=(1,), padding=((k - 1, 0),),
        dimension_numbers=('NWC', 'WIO', 'NWC'), feature_group_count=c)

def _gated_delta_rule(q, k, v, g, beta):
    b, s, h, dk = q.shape
    dv = v.shape[-1]
    c = GDN_CHUNK
    n = s // c

    def chunk(t):
        return t.reshape(b, n, c, h, -1).transpose(0, 3, 1, 2, 4)

    qc, kc, vc = chunk(q), chunk(k), chunk(v)
    gc = g.reshape(b, n, c, h).transpose(0, 3, 1, 2)
    bc = beta.reshape(b, n, c, h).transpose(0, 3, 1, 2)
    G = jnp.cumsum(gc, axis=-1)
    causal = jnp.tril(jnp.ones((c, c), dtype=bool))
    strict = jnp.tril(jnp.ones((c, c), dtype=bool), k=-1)
    decay_incl = jnp.exp(jnp.where(causal, G[..., :, None] - G[..., None, :], -jnp.inf))
    decay_strict = jnp.where(strict, decay_incl, 0.0)
    k_beta = kc * bc[..., None]
    a = jnp.einsum('bhnid,bhnjd->bhnij', k_beta, kc) * decay_strict
    eye = jnp.eye(c, dtype=a.dtype)
    t_inv = lax.linalg.triangular_solve(eye + a, jnp.broadcast_to(eye, a.shape),
                                        left_side=True, lower=True, unit_diagonal=True)
    u = t_inv @ (vc * bc[..., None])
    w = t_inv @ (k_beta * jnp.exp(G)[..., None])
    attn = jnp.einsum('bhnid,bhnjd->bhnij', qc, kc) * decay_incl
    q_dec = qc * jnp.exp(G)[..., None]
    g_last = G[..., -1:]
    k_dec = kc * jnp.exp(g_last - G)[..., None]
    chunk_decay = jnp.exp(g_last[..., 0])
    xs = tuple(jnp.moveaxis(t, 2, 0) for t in (q_dec, attn, u, w, k_dec, chunk_decay))

    def step(state, inp):
        q_e, at, u_c, w_c, k_d, dec = inp
        v_new = u_c - jnp.einsum('bhck,bhkv->bhcv', w_c, state)
        o = jnp.einsum('bhck,bhkv->bhcv', q_e, state) + jnp.einsum('bhij,bhjv->bhiv', at, v_new)
        state = state * dec[..., None, None] + jnp.einsum('bhck,bhcv->bhkv', k_d, v_new)
        return state, o

    state0 = jnp.zeros((b, h, dk, dv), dtype=q.dtype)
    _, o = lax.scan(step, state0, xs)
    return o.transpose(1, 0, 3, 2, 4).reshape(b, s, h, dv)

def second_inputs(seed: int = 0) -> dict:
    key = jax.random.key(seed)
    ks = jax.random.split(key, 12)
    f32 = jnp.float32
    x = jax.random.normal(ks[0], (BATCH, SEQ, D_MODEL), f32)
    norm_w = 1.0 + 0.05 * jax.random.normal(ks[1], (DEPTH_2, D_MODEL), f32)
    w_in = jax.random.normal(ks[2], (DEPTH_2, D_MODEL, IN_WIDTH), f32) * D_MODEL ** -0.5
    conv_w = jax.random.normal(ks[3], (DEPTH_2, GDN_CONV, 2 * GDN_K_WIDTH + GDN_V_WIDTH), f32) * GDN_CONV ** -0.5
    a_log = jnp.log(jax.random.uniform(ks[4], (DEPTH_2, GDN_HEADS), f32, 1.0, 16.0))
    dt_bias = 0.5 * jax.random.normal(ks[5], (DEPTH_2, GDN_HEADS), f32)
    gdn_norm_w = 1.0 + 0.05 * jax.random.normal(ks[6], (DEPTH_2, GDN_VAL_DIM), f32)
    w_up_a = jax.random.normal(ks[7], (DEPTH_2, DSA_WIDTH, D_MODEL), f32) * DSA_WIDTH ** -0.5
    w_up_b = jax.random.normal(ks[8], (DEPTH_2, GDN_V_WIDTH, D_MODEL), f32) * GDN_V_WIDTH ** -0.5
    w_out = jax.random.normal(ks[9], (DEPTH_2, D_MODEL, D_MODEL), f32) * D_MODEL ** -0.5
    final_norm_w = 1.0 + 0.05 * jax.random.normal(ks[10], (D_MODEL,), f32)
    return {'x': x, 'norm_w': norm_w, 'w_in': w_in, 'conv_w': conv_w, 'a_log': a_log,
            'dt_bias': dt_bias, 'gdn_norm_w': gdn_norm_w, 'w_up_a': w_up_a, 'w_up_b': w_up_b,
            'w_out': w_out, 'final_norm_w': final_norm_w}

def second_block(x, norm_w, w_in, conv_w, a_log, dt_bias, gdn_norm_w, w_up_a, w_up_b, w_out, final_norm_w):
    f32 = jnp.float32
    b, s, _ = x.shape
    cos, sin = _rope_tables(s, DSA_HEAD_DIM)
    for layer in range(DEPTH_2):
        h = _rmsnorm(x, norm_w[layer])
        proj = h @ w_in[layer]
        dsa_qkv, dsa_z, gdn_qkv, gdn_z, gdn_b, gdn_a, gate_a, gate_b = _split_columns(proj)

        qkv = dsa_qkv.astype(f32).reshape(b, s, DSA_GROUPS, 3, DSA_HEADS, DSA_HEAD_DIM)
        q_a = _apply_rope(qkv[:, :, :, 0], cos, sin)
        k_a = _apply_rope(qkv[:, :, :, 1], cos, sin)
        v_a = qkv[:, :, :, 2]
        o_a = _dilated_mixture(q_a, k_a, v_a).astype(x.dtype)
        y_a = (o_a * jax.nn.silu(dsa_z)) @ w_up_a[layer]

        cqkv = jax.nn.silu(_causal_depthwise_conv(gdn_qkv, conv_w[layer])).astype(f32)
        gq, gk, gv = jnp.split(cqkv, [GDN_K_WIDTH, 2 * GDN_K_WIDTH], axis=-1)
        gq = _l2norm(gq.reshape(b, s, GDN_HEADS, GDN_KEY_DIM)) * GDN_KEY_DIM ** -0.5
        gk = _l2norm(gk.reshape(b, s, GDN_HEADS, GDN_KEY_DIM))
        gv = gv.reshape(b, s, GDN_HEADS, GDN_VAL_DIM)
        beta = jax.nn.sigmoid(gdn_b.astype(f32))
        g = -jnp.exp(a_log[layer].astype(f32)) * jax.nn.softplus(gdn_a.astype(f32) + dt_bias[layer].astype(f32))
        o_b = _gated_delta_rule(gq, gk, gv, g, beta)
        o_b = _rmsnorm(o_b, gdn_norm_w[layer]).reshape(b, s, GDN_V_WIDTH).astype(x.dtype)
        y_b = (o_b * jax.nn.silu(gdn_z)) @ w_up_b[layer]

        merged = jax.nn.sigmoid(gate_a) * y_a + jax.nn.sigmoid(gate_b) * y_b
        x = x + merged @ w_out[layer]
    return _rmsnorm(x, final_norm_w)


def setup_inputs(seed=0):
    out = dict(first_inputs(seed))
    for name, value in second_inputs(seed + 1).items():
        if name != "x":
            out[name + "_2"] = value
    return out


def reference(
    x, c, w_ada, b_ada, g_ffn1, w_ffn1_in, w_ffn1_out, g_mix, w_mix_in, w_mix_out, att_q_gain,
    att_k_gain, att_sinks, rwkv_mu, rwkv_w0, rwkv_w_w2, rwkv_a0, rwkv_a_w2, rwkv_g_w2, rwkv_k_k,
    rwkv_k_a, rwkv_r_k, rwkv_gn_w, rwkv_gn_b, conv_w, g_ffn2, w_ffn2_in, w_ffn2_out, norm_w_2,
    w_in_2, conv_w_2, a_log_2, dt_bias_2, gdn_norm_w_2, w_up_a_2, w_up_b_2, w_out_2,
    final_norm_w_2,
):
    x = first_block(
        x, c, w_ada, b_ada, g_ffn1, w_ffn1_in, w_ffn1_out, g_mix, w_mix_in, w_mix_out,
        att_q_gain, att_k_gain, att_sinks, rwkv_mu, rwkv_w0, rwkv_w_w2, rwkv_a0, rwkv_a_w2,
        rwkv_g_w2, rwkv_k_k, rwkv_k_a, rwkv_r_k, rwkv_gn_w, rwkv_gn_b, conv_w, g_ffn2,
        w_ffn2_in, w_ffn2_out,
    )
    return second_block(
        x, norm_w_2, w_in_2, conv_w_2, a_log_2, dt_bias_2, gdn_norm_w_2, w_up_a_2, w_up_b_2,
        w_out_2, final_norm_w_2,
    )


_drawn_inputs = setup_inputs


def setup_inputs(seed=0):
    import zlib

    import numpy as np

    out = dict(_drawn_inputs(seed))
    spreads = {}
    factors = {'att_q_gain': 6.126,
     'att_k_gain': 6.606,
     'att_sinks': 3.67,
     'rwkv_w_w2': 8.0,
     'rwkv_a0': 3.192,
     'rwkv_a_w2': 3.246,
     'rwkv_gn_w': 3.021,
     'rwkv_gn_b': 8.0,
     'gdn_norm_w_2': 6.229,
     'w_up_a_2': 2.825}
    for name, (base, spread) in spreads.items():
        noise = np.random.default_rng([zlib.crc32(name.encode()), seed]).standard_normal(out[name].shape)
        drawn = base * np.exp(spread * noise) if base else spread * noise
        out[name] = jnp.asarray(drawn.astype(out[name].dtype))
    for name, factor in factors.items():
        out[name] = (out[name] * factor).astype(out[name].dtype)
    return out
```

```python
import math
from contextlib import ExitStack

import concourse.bass as bass
from concourse import mybir

F32 = mybir.dt.float32
F32R = mybir.dt.float32r
ALU = mybir.AluOpType
ACT = mybir.ActivationFunctionType
AX = mybir.AxisListType

P = 128
T = 512
D = 1024
KD = D // P
DFF = 2816
NF = DFF // P
HALF = NF // 2
DEPTH = 2
NMOD = 9
EPS = 1e-6
WIDE = 2 * KD * P
TALL = HALF * P
ADA_COLS = 256
ADA_PIECES = NMOD * D // ADA_COLS
ADA_FIRST = 2 * D // ADA_COLS
ADA_BATCHES = {0: (ADA_FIRST, ADA_FIRST + 8, ADA_PIECES), 1: (0, 12, ADA_PIECES)}


def steps(eng, n, body):
    if n == 1:
        return body(0, 0)
    body(0, 0)
    pairs = (n - 2) // 2
    if pairs > 1:
        with eng.Fori(0, pairs) as i:
            body(2 * i + 1, 1)
            body(2 * i + 2, 0)
    elif pairs == 1:
        body(1, 1)
        body(2, 0)
    for idx in range(1 + 2 * pairs, n):
        body(idx, idx % 2)


class Unit:

    def __init__(self, x, y, v1, bt, mb, rhs, u, mc=None, w1=None):
        self.x, self.y = x, y
        self.v1, self.bt = v1, bt
        self.mb, self.mc = mb, mc
        self.w1, self.rhs, self.u = w1, rhs, u


class Chain:

    def __init__(self, eng, sem):
        self.eng, self.sem, self.n = eng, sem, 0

    def __call__(self, ins):
        self.n += 1
        ins.then_inc(self.sem, 1)
        self.eng.wait_ge(self.sem, self.n)

ARENA = 23552
TT = ARENA // T
HD = 64
NB = T // P
PAIRS = 4
MIX_TILES = 20
DECAY_RATE = math.exp(-0.5)
GN_EPS = 64e-5
LEVELS = range(2, 7)
V1_BANK, X_BANK, Y_BANK = (2, 0), (4, 6), (5, 7)
NEG = -1e30
VEC = {"mu": 8, "w0": 2, "a0": 2, "k_k": 2, "k_a": 2, "r_k": 2, "gn_w": 2, "gn_b": 2, "conv": 6, "q_gain": 1, "k_gain": 1}
VEC_AT = {k: sum(list(VEC.values())[:i]) for i, k in enumerate(VEC)}
NVEC = sum(VEC.values())


LAYERS = DEPTH
G0 = LAYERS * NB
S0 = LAYERS * (2 * NB + 1)
A0 = LAYERS * 8
MERGE = (KD + 4) * P
DILATION = (1, 4, 16)
VEC2 = {"norm": 8, "final": 8, "conv": 48, "gdn_norm": 1, "a_log": 1, "dt": 1}
VEC2_AT = {k: sum(list(VEC2.values())[:i]) for i, k in enumerate(VEC2)}
NVEC2 = sum(VEC2.values())
POOL_MIX = 21


def program(nc, w, out):
    phases = []
    for l in range(LAYERS):
        for f in (2 * l, 2 * l + 1):
            if f % 2:
                phases.append(("mix_in", (l, 0), MIX_TILES // 2, WIDE))
                phases.append(("mix_out", (l, 0), KD // 2, WIDE))
            for half in range(2):
                phases.append(("up", (f, half), HALF, WIDE))
                phases.append(("down", (f, half), KD, TALL))
    phases += [("gdn_in", 0, 6, WIDE), ("gdn_ba", 0, 1, KD * P), ("gdn_z", 0, 2, WIDE)]
    phases += [("dsa_in", g, 6, WIDE) for g in range(3)]
    phases += [("dsa_z", 0, 2, WIDE), ("merge", 0, KD, MERGE), ("merge", 1, KD, MERGE), ("last", 0, 4, WIDE)]
    starts = [sum(p[2] for p in phases[:i]) for i in range(len(phases) + 1)]
    start_of = {(p[0], p[1]): s for p, s in zip(phases, starts)}

    def size_of(piece):
        for p, s in zip(phases, starts):
            if s <= piece < s + p[2]:
                return p[3]
        return None

    with ExitStack() as ctx:
        def sb(name, shape, dt=F32):
            return ctx.enter_context(nc.sbuf_tensor(name, shape, dt))

        def sem(name):
            return ctx.enter_context(nc.semaphore(name))

        h = sb("h", [P, KD, T])
        hn_hi = sb("hn_hi", [P, KD, T], F32R)
        hn_lo = sb("hn_lo", [P, KD, T], F32R)
        w_raw = sb("w_raw", [P, 2, WIDE])
        w_hi = sb("w_hi", [P, 2, WIDE], F32R)
        w_lo = sb("w_lo", [P, 2, WIDE], F32R)
        arena_at = -(-nc.sbuf_base // 32) * 32
        sb("arena", [P, ARENA + 8])
        ones = sb("ones", [P, P])
        eps = sb("eps", [P, 1])
        rstd_at = -(-nc.sbuf_base // 32) * 32
        rstd = sb("rstd", [P, T])
        tmp_at = -(-nc.sbuf_base // 32) * 32
        tmp = sb("tmp", [P, 2, T])
        mod = sb("mod", [P, NMOD * KD])
        b_ada = sb("b_ada", [P, DEPTH, NMOD * KD])
        gains = sb("gains", [P, DEPTH, 3, KD])
        cvec = sb("cvec", [P, KD])
        csig = sb("csig", [P, KD])
        norm_gain = sb("norm_gain", [P, KD])
        out_gain = sb("out_gain", [P, KD])

        def place(name, shape, dt=F32):
            n = 1
            for x in shape[1:]:
                n *= x
            tensor = nc.alloc_sbuf_tensor_at(name, shape, dt, offset=arena_at + 4 * used[0])
            used[0] += n
            assert used[0] <= ARENA, (name, used[0])
            return tensor

        def tiles(name, first, count, shape=None, dt=F32):
            used[0] = first * T
            assert first + count <= TT, name
            return place(name, shape or [P, count, T], dt)

        used = [0]
        act_hi = place("act_hi", [P, HALF, T], F32R)
        act_lo = place("act_lo", [P, HALF, T], F32R)
        silu = place("silu", [P, 2, T])
        act_f = place("act_f", [P, 2, T])
        ada_w = place("ada_w", [P, 2, KD, ADA_COLS])
        ada_acc = place("ada_acc", [P, 24 * ADA_COLS])
        used = [0]
        ada_first = place("ada_first", [P, ADA_FIRST, KD, ADA_COLS])

        proj = tiles("proj", 0, MIX_TILES)
        att_r = tiles("att_r", 20, 5)
        att_s = tiles("att_s", 25, 4, [P, 2, 4, 256])
        att_p = tiles("att_p", 29, 2)
        att_v = tiles("att_v", 31, 1, [P, NB, P])
        shift = tiles("shift", 32, 8)
        conv_u = tiles("conv_u", 40, 2)
        conv_t = tiles("conv_t", 42, 1)
        conv_y = tiles("conv_y", 43, 2)
        rw_bi = tiles("rw_bi", 0, 2)
        rw_r = tiles("rw_r", 2, 2)
        rw_ls = tiles("rw_ls", 4, 2)
        rw_sw = tiles("rw_sw", 20, 2)
        rw_a = tiles("rw_a", 22, 2)
        rw_g = tiles("rw_g", 24, 2)
        rw_kk = tiles("rw_kk", 26, 2)
        rw_kr = tiles("rw_kr", 28, 4, [P, 2, 2, T])
        rw_ki = tiles("rw_ki", 32, 2)
        rw_ed = tiles("rw_ed", 34, 2)
        rw_bonus = tiles("rw_bonus", 36, 2)
        rw_vt = tiles("rw_vt", 38, 2, [P, 2, NB, P])
        rw_bt = tiles("rw_bt", 40, 2, [P, 2, NB, P])
        rw_kt = tiles("rw_kt", 14, 2, [P, 2, NB, P])
        rw_y = tiles("rw_y", 16, 2)
        lora = tiles("lora", 45, 1, [P, 2, 2 * P])
        d_x = tiles("d_x", 18, 1, [P, 2, 2, P])
        d_y = tiles("d_y", 19, 1, [P, 2, 2, P])
        d_v1 = tiles("d_v1", 12, 1, [P, 2, 2, P])
        d_bt = tiles("d_bt", 20, 2, [P, 2, 2, 2, P])
        d_mb = tiles("d_mb", 42, 2, [P, 2, 2, 2, P])
        d_mc = tiles("d_mc", 26, 2, [P, 2, 2, 2, P])
        d_w1 = tiles("d_w1", 4, 1, [P, 2, P])
        d_rhs = tiles("d_rhs", 5, 1, [P, 2, P])
        d_u = tiles("d_u", 45, 1, [P, 2, P])

        rwu = Unit(x=d_x, y=d_y, v1=d_v1, bt=d_bt, mb=d_mb, mc=d_mc, w1=d_w1, rhs=d_rhs, u=d_u)
        gd_raw = tiles("gd_raw", 0, 12)
        gd_kq = tiles("gd_kq", 0, 8, [P, 2, PAIRS, T])
        gd_kbg = tiles("gd_kbg", 8, 4)
        gd_conv_out = tiles("gd_conv_out", 12, 12)
        gd_q, gd_k, gd_v = (gd_conv_out[:, 4 * i:4 * i + 4] for i in range(3))
        gd_qd = tiles("gd_qd", 12, 4)
        gd_y = tiles("gd_y", 20, 4)
        gd_z = tiles("gd_z", 12, 4)
        sel_head = tiles("sel_head", 24, 2, [P, 8, P])
        sel_pair = tiles("sel_pair", 26, 1, [P, PAIRS, P])
        gd_rows = tiles("gd_rows", 27, 1 + 2, [P, 3, T])
        gd_kd = tiles("gd_kd", 29, 4)
        gd_vt = tiles("gd_vt", 33, 4, [P, PAIRS, NB, P])
        gd_kt = tiles("gd_kt", 37, 4, [P, PAIRS, NB, P])
        gdu = Unit(x=tiles("gd_x", 29, 1, [P, 2, 2, P]), y=tiles("gd_yi", 30, 1, [P, 2, 2, P]), v1=tiles("gd_v1", 31, 1, [P, 2, 2, P]),
                   bt=tiles("gd_bt", 41, 2, [P, 2, 2, 2, P]), mb=tiles("gd_mb", 43, 2, [P, 2, 2, 2, P]), rhs=tiles("gd_rhs", 45, 1, [P, 2, P]),
                   u=place("gd_u", [P, 2, P]))
        gd_e = tiles("gd_e", 32, 1, [P, 2, 2, P])
        yb_hi = tiles("yb_hi", 38, 4, dt=F32R)
        yb_lo = tiles("yb_lo", 42, 4, dt=F32R)
        ds_qkv = tiles("ds_qkv", 0, 12)
        ds_s = tiles("ds_s", 12, 4, [P, 2, 4, 256])
        ds_t = tiles("ds_t", 12, 4)
        ds_p = tiles("ds_p", 16, 2)
        ds_table = tiles("ds_table", 18, 2)
        ds_o = [tiles("ds_o0", 32, 4), tiles("ds_o1", 20, 4), tiles("ds_o2", 24, 4)]
        ds_v = tiles("ds_v", 28, 4, [P, PAIRS, NB, P])
        ds_mask = tiles("ds_mask", 36, 1, [P, 3 * P])
        turn_half = place("turn_half", [P, P])
        sel_mix = tiles("sel_mix", 37, 1, [P, PAIRS, P])
        ds_z = tiles("ds_z", 0, 4)
        ds_rows = tiles("ds_rows", 4, 7)
        ya_hi = tiles("ya_hi", 12, 4, dt=F32R)
        ya_lo = tiles("ya_lo", 16, 4, dt=F32R)
        mg = tiles("mg", 0, 8)
        mg_g = tiles("mg_g", 8, 2)

        vec2 = sb("vec2", [P, NVEC2])
        gd_neglog = sb("gd_neglog", [P, NB, 8])
        gd_decay = sb("gd_decay", [P, PAIRS, 2 * NB])
        gd_ends = sb("gd_ends", [P, PAIRS * 2 * NB])
        pool_mark = sb("pool_mark", [P, 1])
        gd_rate = sb("gd_rate", [P, 1])
        ds_stat = sb("ds_stat", [P, 3, 2, NB, 8])

        def v2(name, j=0, n=1):
            at = VEC2_AT[name] + j
            return vec2[:, at:at + n]

        ident = sb("ident", [P, P])
        blk = sb("blk", [P, P])
        band = sb("band", [P, 2 * P])
        up_mask = sb("up_mask", [P, 2, P])
        pair_low = sb("pair_low", [P, P])
        level = sb("level", [P, 6, P])
        restart = sb("restart", [P, T])
        vec = sb("vec", [P, DEPTH, NVEC])
        sinks = sb("sinks", [P, DEPTH, 8])
        att_mx = sb("att_mx", [P, 2, 4])
        att_nm = sb("att_nm", [P, 2, 4])
        att_dd = sb("att_dd", [P, 2, 4])
        att_den = sb("att_den", [P, 2, 4])
        att_es = sb("att_es", [P, 2, 4])
        chunk_decay = sb("chunk_decay", [P, 2, 2 * NB])
        state = nc.alloc_sbuf_tensor_at("state", [P, PAIRS, P], F32, offset=rstd_at)
        state_p = nc.alloc_sbuf_tensor_at("state_p", [P, PAIRS, P], F32, offset=tmp_at)
        gn_eps = sb("gn_eps", [P, 1])

        ps = ctx.enter_context(nc.psum_tensor("ps", [P, 8, T], F32))
        main = [[ps[:, 2 * s + t] for t in range(2)] for s in range(2)]
        small = [ps[:, 4 + s] for s in range(4)]
        dsa_tables = sem("dsa_tables")
        lora_loaded = sem("lora_loaded")
        vec2_loaded = sem("vec2_loaded")
        vec_loaded = sem("vec_loaded")
        dsa_masks = sem("dsa_masks")
        gd_masks = sem("gd_masks")
        mask_step = sem("mask_step")
        masks_ready = sem("masks_ready")
        att_exp = sem("att_exp")
        att_masked = sem("att_masked")
        att_max = sem("att_max")
        att_out = sem("att_out")
        att_out_hi = sem("att_out_hi")
        att_p_ready = sem("att_p_ready")
        att_probs = sem("att_probs")
        att_pv = sem("att_pv")
        att_scored = sem("att_scored")
        att_turned = sem("att_turned")
        att_v_ready = sem("att_v_ready")
        att_v_turned = sem("att_v_turned")
        qk_normed = sem("qk_normed")
        qk_roots = sem("qk_roots")
        qk_squared = sem("qk_squared")
        qk_sums = sem("qk_sums")
        bonus_raw = sem("bonus_raw")
        bonus_sums = sem("bonus_sums")
        conv_hi = sem("conv_hi")
        conv_ready = sem("conv_ready")
        decays_ready = sem("decays_ready")
        factors_ready = sem("factors_ready")
        gates_ready = sem("gates_ready")
        gn_centred = sem("gn_centred")
        gn_roots = sem("gn_roots")
        gn_square_sums = sem("gn_square_sums")
        gn_squared = sem("gn_squared")
        gn_sums = sem("gn_sums")
        kk_norms = sem("kk_norms")
        kk_raw = sem("kk_raw")
        kk_squared = sem("kk_squared")
        kk_sums = sem("kk_sums")
        logs_ready = sem("logs_ready")
        lora_out = sem("lora_out")
        lora_ready = sem("lora_ready")
        mix_pool_own = sem("mix_pool_own")
        mixed_ready = sem("mixed_ready")
        rw_out = sem("rw_out")
        rw_out_hi = sem("rw_out_hi")
        rw_tokens_a = sem("rw_tokens_a")
        rw_tokens_b = sem("rw_tokens_b")
        rw_turned = sem("rw_turned")
        shifted = sem("shifted")
        delta_bt_ready = sem("delta_bt_ready")
        delta_masked = sem("delta_masked")
        delta_mats = sem("delta_mats")
        delta_o_ready = sem("delta_o_ready")
        delta_o_summed = sem("delta_o_summed")
        delta_q_summed = sem("delta_q_summed")
        delta_rhs_ready = sem("delta_rhs_ready")
        delta_s_summed = sem("delta_s_summed")
        delta_state = sem("delta_state")
        delta_u_ready = sem("delta_u_ready")
        delta_u_summed = sem("delta_u_summed")
        delta_v1_ready = sem("delta_v1_ready")
        delta_v1_summed = sem("delta_v1_summed")
        delta_w1_ready = sem("delta_w1_ready")
        delta_w1_summed = sem("delta_w1_summed")
        delta_y_ready = sem("delta_y_ready")
        delta_x_ready = sem("delta_x_ready")
        delta_xy_summed = sem("delta_xy_summed")
        gd_conv = sem("gd_conv")
        gd_e_ready = sem("gd_e_ready")
        gd_exp_log = sem("gd_exp_log")
        gd_exp_to_end = sem("gd_exp_to_end")
        gd_log_ready = sem("gd_log_ready")
        gd_log_spread = sem("gd_log_spread")
        gd_log_turned = sem("gd_log_turned")
        gd_normed = sem("gd_normed")
        gd_roots = sem("gd_roots")
        gd_rows_ready = sem("gd_rows_ready")
        gd_softplus = sem("gd_softplus")
        gd_spread = sem("gd_spread")
        gd_spread_read = sem("gd_spread_read")
        gd_squared = sem("gd_squared")
        gd_sums = sem("gd_sums")
        gd_taken_ready = sem("gd_taken_ready")
        gd_to_end = sem("gd_to_end")
        gd_tokens_a = sem("gd_tokens_a")
        gd_tokens_b = sem("gd_tokens_b")
        gd_turned = sem("gd_turned")
        gd_y_ready = sem("gd_y_ready")
        gd_y_roots = sem("gd_y_roots")
        gd_y_squared = sem("gd_y_squared")
        gd_y_sums = sem("gd_y_sums")
        yb_high = sem("yb_high")
        yb_ready = sem("yb_ready")
        dsa_exp_shifted = sem("dsa_exp_shifted")
        dsa_mixed = sem("dsa_mixed")
        dsa_roped = sem("dsa_roped")
        dsa_rot_read = sem("dsa_rot_read")
        dsa_rotated = sem("dsa_rotated")
        dsa_rows = sem("dsa_rows")
        dsa_shifted = sem("dsa_shifted")
        dsa_stat_turned = sem("dsa_stat_turned")
        dsa_v_ready = sem("dsa_v_ready")
        dsa_v_turned = sem("dsa_v_turned")
        dsa_weights = sem("dsa_weights")
        dsa_weights_spread = sem("dsa_weights_spread")
        dsa_z_ready = sem("dsa_z_ready")
        ya_f_ready = sem("ya_f_ready")
        ya_high = sem("ya_high")
        ya_ready = sem("ya_ready")
        merged = sem("merged")
        merged_hi = sem("merged_hi")
        mg_step = sem("mg_step")
        const_ready = sem("const_ready")
        small_loaded = sem("small_loaded")
        x_loaded = sem("x_loaded")
        c_ready = sem("c_ready")
        raw_loaded = [sem("raw_loaded0"), sem("raw_loaded1")]
        w_hi_ready = sem("w_hi_ready")
        w_lo_ready = sem("w_lo_ready")
        piece_done = sem("piece_done")
        act_evac = sem("act_evac")
        dve_evac = sem("dve_evac")
        act_f_ready = sem("act_f_ready")
        act_hi_ready = sem("act_hi_ready")
        act_lo_ready = sem("act_lo_ready")
        sq_ready = sem("sq_ready")
        sq_summed = sem("sq_summed")
        norm_sqrt = sem("norm_sqrt")
        hn_tmp = sem("hn_tmp")
        hn_hi_ready = sem("hn_hi_ready")
        hn_ready = sem("hn_ready")
        ada_first_loaded = sem("ada_first_loaded")
        ada_loaded = [sem("ada_loaded0"), sem("ada_loaded1")]
        ada_done = sem("ada_done")
        ada_summed = sem("ada_summed")
        pool_own = sem("pool_own")
        dve_own = sem("dve_own")
        act_own = sem("act_own")
        stored = sem("stored")
        h_final = sem("h_final")

        block = ctx.enter_context(nc.Block())

        flushes = [(0, 0, ADA_FIRST)] + [(l, a, b) for l in range(DEPTH) for a, b in
                                         zip(ADA_BATCHES[l], ADA_BATCHES[l][1:])]
        ada_batch = {(f, i): 1 + 2 * f + i for f in range(2) for i in range(2)}

        def vcol(l, name, j=0):
            at = VEC_AT[name] + j
            return vec[:, l, at:at + 1]

        def over(ap, shape):
            return ap.broadcast_to(shape)

        def delta_pool(pool, d, g):
            pool.wait_ge(delta_masked, g + 1)
            for m, lv in enumerate(LEVELS):
                n = len(LEVELS) * g + m
                if n >= 2:
                    pool.wait_ge(delta_v1_summed, 2 * (n - 1))
                pool.tensor_tensor(d.bt[:, m % 2], d.mb[:, :, :, 0], level[:, lv - 1].unsqueeze(1).unsqueeze(1).broadcast_to([P, 2, 2, P]),
                                   ALU.mult).then_inc(delta_bt_ready, 1)

        @block.sync
        def _(sp):
            sp.dma_start(cvec[:], w["c"]).then_inc(small_loaded, 16)
            sp.dma_start(b_ada[:], w["b_ada"]).then_inc(small_loaded, 16)
            sp.dma_start(gains[:], w["gains"]).then_inc(small_loaded, 16)
            for q in range(ADA_FIRST if LAYERS else 0):
                sp.dma_start(ada_first[:, q], w["ada"][0, q]).then_inc(ada_first_loaded, 16)
            sp.dma_start(h[:], w["x"]).then_inc(x_loaded, 16)
            sp.dma_start(vec[:], w["vec"]).then_inc(vec_loaded, 16)
            sp.dma_start(vec2[:], w["vec2"]).then_inc(vec2_loaded, 16)
            sp.dma_start(sinks[:], w["sinks"].broadcast_to([P, DEPTH, 8])).then_inc(vec_loaded, 16)
            for (kind, at, n, size), p0 in zip(phases, starts):
                def load(i, odd):
                    slot = (p0 + odd) % 2
                    if not (isinstance(i, int) and p0 + i < 2):
                        sp.wait_ge(w_lo_ready, p0 + i - 1)
                    sp.dma_start(w_raw[:, slot, 0:size], w[kind](at, i)).then_inc(raw_loaded[slot], 16)
                steps(sp, n, load)
                if kind == "mix_in":
                    sp.wait_ge(piece_done, p0 + 1)
                    sp.dma_start(lora[:], w["lora"][:, at[0]]).then_inc(lora_loaded, 16)
                if kind == "dsa_in":
                    if at:
                        sp.wait_ge(dsa_roped, 2 * at)
                    else:
                        sp.wait_ge(delta_o_ready, G0 + 2 * NB)
                    sp.dma_start(ds_table[:], w["rope"][:, at]).then_inc(dsa_tables, 16)
            sp.wait_ge(h_final, 1)
            sp.dma_start(out, mg[:]).then_inc(stored, 16)
            sp.wait_ge(stored, 16)

        @block.gpsimd
        def _(pool):
            def select(out_, pattern, base, cm, op, fill=0.0):
                pool.affine_select(out_, out_, pattern, op, fill, base=base, channel_multiplier=cm).then_inc(mask_step, 1)
                nstep[0] += 1
                pool.wait_ge(mask_step, nstep[0])

            def fill(ap, value):
                pool.memset(ap, value).then_inc(mask_step, 1)
                nstep[0] += 1
                pool.wait_ge(mask_step, nstep[0])

            nstep = [0]

            def make_masks(pool):
                chunked = [[-HD, 2], [0, HD]]
                fill(ident[:], 0.0)
                select(ident[:], [[-1, P]], 0, 1, ALU.not_equal, 1.0)
                fill(gn_eps[:], GN_EPS)
                fill(blk[:], 1.0)
                select(blk[:].rearrange("p (c i) -> p c i", c=2), chunked, 0, 1, ALU.is_ge)
                select(blk[:].rearrange("p (c i) -> p c i", c=2), [[HD, 2], [0, HD]], HD - 1, -1, ALU.is_ge)
                fill(band[:], 0.0)
                select(band[:], [[-1, 2 * P]], P, 1, ALU.is_ge, NEG)
                select(band[:], [[1, 2 * P]], 0, -1, ALU.is_gt, NEG)
                fill(up_mask[:], 1.0)
                for which, op in ((0, ALU.is_gt), (1, ALU.is_ge)):
                    m = up_mask[:, which].rearrange("p (c i) -> p c i", c=2)
                    select(m, [[HD, 2], [1, HD]], 0, -1, op)
                    select(m, chunked, 0, 1, ALU.is_ge)
                fill(pair_low[:], 0.0)
                m = pair_low[:].rearrange("p (b x) -> p b x", x=2)[:, :, 0]
                fill(m, 1.0)
                select(m, [[-2, P // 2]], -1, 1, ALU.is_equal)
                fill(level[:], 0.0)
                for lv in range(1, 7):
                    n = 1 << (lv - 1)
                    m = level[:, lv - 1].rearrange("p (b x i) -> p b x i", x=2, i=n)[:, :, 1]
                    fill(m, 1.0)
                    select(m, [[-2 * n, P // (2 * n)], [0, n]], 0, 1, ALU.is_ge)
                    select(m, [[2 * n, P // (2 * n)], [0, n]], n, -1, ALU.is_gt)
                fill(restart[:], 1.0)
                fill(restart[:].rearrange("p (c i) -> p c i", i=HD)[:, :, 0], 0.0)
                pool.memset(pool_mark[:], 0.0).then_inc(masks_ready, 1)

            def mix_pool(pool, l):
                v = l + 1
                n = [0]

                def own(ins):
                    n[0] += 1
                    ins.then_inc(mix_pool_own, 1)
                    pool.wait_ge(mix_pool_own, POOL_MIX * l + n[0])

                p_end = start_of["mix_in", (l, 0)] + MIX_TILES // 2
                if l == 0:
                    pool.wait_ge(vec_loaded, 32)
                pool.wait_ge(act_evac, p_end)
                pool.wait_ge(dve_evac, p_end)
                pr = proj[:, 6:14]
                own(pool.tensor_tensor(shift[:, :, 1:T], pr[:, :, 0:T - 1], pr[:, :, 1:T], ALU.subtract))
                own(pool.tensor_scalar(shift[:, :, 0:1], pr[:, :, 0:1], -1.0, None, ALU.mult))
                for j in range(8):
                    own(pool.tensor_scalar(shift[:, j], shift[:, j], vcol(l, "mu", j), None, ALU.mult))
                pool.tensor_tensor(pr, pr, shift[:], ALU.add).then_inc(shifted, 1)
                own(pool.tensor_tensor(conv_u[:], proj[:, 16:18], proj[:, 18:20], ALU.mult))
                for j in range(2):
                    own(pool.tensor_scalar(conv_y[:, j], conv_u[:, j], vcol(l, "conv", 4 + j), None, ALU.mult))
                    for back in (1, 2):
                        own(pool.tensor_scalar(conv_t[:, 0], conv_u[:, j], vcol(l, "conv", 2 * (2 - back) + j), None, ALU.mult))
                        own(pool.tensor_tensor(conv_y[:, j, back:T], conv_y[:, j, back:T], conv_t[:, 0, 0:T - back], ALU.add))
                pool.tensor_tensor(conv_y[:], conv_y[:], proj[:, 14:16], ALU.mult).then_inc(conv_ready, 1)
                assert n[0] == POOL_MIX, n
                for u in range(NB):
                    delta_pool(pool, rwu, l * NB + u)

            pool.memset(ones[:], 1.0).then_inc(const_ready, 1)
            pool.memset(eps[:], EPS).then_inc(const_ready, 1)
            def second_pool(pool):
                p0 = start_of["gdn_in", 0]
                if p0:
                    pool.wait_ge(dve_evac, p0)
                    pool.wait_ge(act_evac, p0)
                fill(sel_head[:], 0.0)
                fill(sel_pair[:], 0.0)
                for first in (0, 32):
                    select(sel_head[:], [[-1, 8], [0, P]], -first, 1, ALU.not_equal, 1.0)
                    select(sel_pair[:].rearrange("p j (h i) -> p j h i", h=2), [[-2, PAIRS], [-1, 2], [0, HD]], -first, 1, ALU.not_equal, 1.0)
                pool.memset(pool_mark[:], 0.0).then_inc(gd_masks, 1)
                for g in range(2 * NB):
                    delta_pool(pool, gdu, G0 + g)
                pool.wait_ge(gd_tokens_a, 1)
                pool.wait_ge(delta_o_ready, G0 + 2 * NB)
                pool.wait_ge(delta_state, S0 + 4 * NB + 1)
                fill(ds_mask[:], 0.0)
                own_block = ds_mask[:, P:2 * P]
                select(ds_mask[:, 0:2 * P], [[-1, 2 * P]], P, 1, ALU.is_ge, NEG)
                select(ds_mask[:, 0:2 * P], [[1, 2 * P]], 0, -1, ALU.is_ge, NEG)
                m = ds_mask[:, 2 * P:3 * P]
                select(m, [[-1, P]], 0, 1, ALU.is_ge, NEG)
                sub = T // DILATION[2]
                m = m.rearrange("p (r i) -> p r i", i=sub)
                select(m, [[sub, P // sub], [0, sub]], sub - 1, -1, ALU.is_ge, NEG)
                fill(turn_half[:], 0.0)
                th = turn_half[:].rearrange("p (h x i) -> p h x i", h=2, x=2)
                select(th[:, :, 0], [[-HD, 2], [-1, HD // 2]], -HD // 2, 1, ALU.not_equal, -1.0)
                select(th[:, :, 1], [[-HD, 2], [-1, HD // 2]], 0, 1, ALU.not_equal, 1.0)
                fill(sel_mix[:], 0.0)
                sm = sel_mix[:].rearrange("p j (h i) -> p j h i", h=2)
                select(sm, [[-1, PAIRS], [-4, 2], [0, HD]], 0, 1, ALU.not_equal, 1.0)
                pool.memset(pool_mark[:], 0.0).then_inc(dsa_masks, 1)

            make_masks(pool)
            pool.wait_ge(c_ready, 2)
            done = 0
            for n, (l, a, b) in enumerate(flushes[1:] if LAYERS else []):
                pool.wait_ge(ada_summed, n + 1)
                if n == 2:
                    pool.wait_ge(mixed_ready, 1)
                for q in range(2):
                    pool.dma_start(ada_w[:, q], w["ada"][l, a + q]).then_inc(ada_loaded[q], 16)
                base = done

                def piece(i, s, more):
                    n_done = base + 2 * i + s
                    own = 3 * n_done
                    pool.wait_ge(ada_loaded[s], 16 * (base // 2 + i + 1))
                    ws = ada_w[:, s]
                    pool.tensor_tensor(ws, ws, cvec[:].unsqueeze(2).broadcast_to([P, KD, ADA_COLS]), ALU.mult).then_inc(pool_own, 1)
                    pool.wait_ge(pool_own, own + 1)
                    pool.tensor_tensor(ws[:, 0:4], ws[:, 0:4], ws[:, 4:8], ALU.add).then_inc(pool_own, 1)
                    pool.wait_ge(pool_own, own + 2)
                    pool.tensor_tensor(ws[:, 0:2], ws[:, 0:2], ws[:, 2:4], ALU.add).then_inc(pool_own, 1)
                    pool.wait_ge(pool_own, own + 3)
                    pool.tensor_tensor(ada_acc[:, bass.ds((2 * i + s) * ADA_COLS, ADA_COLS)], ws[:, 0], ws[:, 1],
                                       ALU.add).then_inc(ada_done, 1)
                    pool.wait_ge(ada_done, n_done + 1)
                    if more:
                        pool.dma_start(ws, w["ada"][l, a + 2 * i + s + 2]).then_inc(ada_loaded[s], 16)

                with pool.Fori(0, (b - a) // 2 - 1) as i:
                    piece(i, 0, True)
                    piece(i, 1, True)
                piece((b - a) // 2 - 1, 0, False)
                piece((b - a) // 2 - 1, 1, False)
                done += b - a
                if n % 2 == 1:
                    mix_pool(pool, n // 2)
            second_pool(pool)

        def pe_flush(pe, n):
            l, a, b = flushes[n]
            if n == 0:
                pe.wait_ge(c_ready, 2)
                pe.wait_ge(ada_first_loaded, 16 * ADA_FIRST)
                for q in range(a, b):
                    for s in range(2):
                        for k in range(KD):
                            last = pe.matmul(small[0][:, 2 * q + s:2 * q + s + 1], ada_first[:, q, k, s * P:(s + 1) * P],
                                             cvec[:, k:k + 1], start=(k == 0), stop=(k == KD - 1))
            else:
                pe.wait_ge(ada_done, sum(x[2] - x[1] for x in flushes[1:n + 1]))
                for q in range(2 * (b - a)):
                    last = pe.matmul(small[0][:, q:q + 1], ada_acc[:, q * P:(q + 1) * P], ones[:, 0:1], start=True, stop=True)
            last.then_inc(ada_summed, 1)

        def dve_flush(dve, own, n):
            l, a, b = flushes[n]
            dve.wait_ge(ada_summed, n + 1)
            if n == 0:
                dve.wait_ge(small_loaded, 48)
            own(dve.tensor_tensor(mod[:, 2 * a:2 * b], small[0][:, 0:2 * (b - a)], b_ada[:, l, 2 * a:2 * b], ALU.add))

        def norm_pe(pe, n):
            for j in range(KD):
                pe.wait_ge(sq_ready, n * KD + j + 1)
                pe.matmul(small[1], ones[:], tmp[:, j % 2], start=(j == 0), stop=(j == KD - 1)).then_inc(sq_summed, 1)

        def norm_act(act, n, shift, last=False):
            for j in range(KD):
                if j >= 2:
                    act.wait_ge(sq_summed, n * KD + j - 1)
                act.activation(tmp[:, j % 2], h[:, j], ACT.Square).then_inc(sq_ready, 1)
            act.wait_ge(sq_summed, n * KD + KD)
            act.activation(rstd[:], small[1], ACT.Sqrt, bias=eps[:], scale=1.0 / D).then_inc(norm_sqrt, 1)
            for j in range(KD if not last else 0):
                act.wait_ge(hn_tmp, n * KD + j + 1)
                if shift is None:
                    act.activation(hn_hi[:, j], tmp[:, j % 2], ACT.Copy).then_inc(hn_hi_ready, 1)
                else:
                    act.activation(hn_hi[:, j], tmp[:, j % 2], ACT.Identity, bias=shift[:, j:j + 1]).then_inc(hn_hi_ready, 1)

        def norm_dve(dve, own, n, gain, scale, shift):
            if scale is None:
                own(dve.tensor_copy(norm_gain[:], gain))
            else:
                own(dve.scalar_tensor_tensor(norm_gain[:], scale, 1.0, gain, ALU.add, ALU.mult))
            dve.wait_ge(norm_sqrt, n + 1)
            own(dve.reciprocal(rstd[:], rstd[:]))

            def low(j):
                dve.wait_ge(hn_hi_ready, n * KD + j + 1)
                if shift is None:
                    dve.tensor_tensor(hn_lo[:, j], tmp[:, j % 2], hn_hi[:, j].bitcast(F32), ALU.subtract).then_inc(hn_ready, 1)
                else:
                    dve.scalar_tensor_tensor(hn_lo[:, j], tmp[:, j % 2], shift[:, j:j + 1], hn_hi[:, j].bitcast(F32),
                                             ALU.add, ALU.subtract).then_inc(hn_ready, 1)
            for j in range(KD):
                if j >= 2:
                    dve.wait_ge(hn_ready, n * KD + j - 1)
                dve.scalar_tensor_tensor(tmp[:, j % 2], h[:, j], norm_gain[:, j:j + 1], rstd[:], ALU.mult,
                                         ALU.mult).then_inc(hn_tmp, 1)
                if j:
                    low(j - 1)
            low(KD - 1)

        def split_act(act, piece, size):
            if size is None:
                return
            slot = piece[1]
            act.wait_ge(raw_loaded[slot], 8 * piece[0] + (16 if slot == 0 else 8))
            if not (isinstance(piece[0], int) and piece[0] < 2):
                act.wait_ge(piece_done, piece[0] - 1)
            act.activation(w_hi[:, slot, 0:size], w_raw[:, slot, 0:size], ACT.Copy).then_inc(w_hi_ready, 1)

        def split_dve(dve, piece, size):
            if size is None:
                return
            slot = piece[1]
            dve.wait_ge(w_hi_ready, piece[0] + 1)
            dve.tensor_tensor(w_lo[:, slot, 0:size], w_raw[:, slot, 0:size], w_hi[:, slot, 0:size].bitcast(F32),
                              ALU.subtract).then_inc(w_lo_ready, 1)

        def ahead(p0, n, size, i, odd):
            piece = p0 + i + 1
            slot = (p0 + odd + 1) % 2
            if isinstance(i, int):
                return (piece, slot), size_of(piece)
            return (piece, slot), size

        def pe_piece(pe, p, slot, K, tiles, x_hi, x_lo, ready):
            pe.wait_ge(w_lo_ready, p + 1)
            if not (isinstance(p, int) and p < 2):
                pe.wait_ge(act_evac, p - 1)
                pe.wait_ge(dve_evac, p - 1)
            for t in range(tiles):
                for k in range(K):
                    if t == 0:
                        ready(k)
                    col = (k * tiles + t) * P
                    wh, wl = w_hi[:, slot, col:col + P], w_lo[:, slot, col:col + P]
                    bank = main[slot][t]
                    pe.matmul(bank, wh, x_hi[:, k], start=(k == 0), stop=False)
                    pe.matmul(bank, wh, x_lo[:, k], start=False, stop=False)
                    last = pe.matmul(bank, wl, x_hi[:, k], start=False, stop=(k == K - 1))
            last.then_inc(piece_done, 1)

        def ffn_pe(pe, f):
            l = f // 2
            n = 3 * l + 2 * (f % 2)
            norm_pe(pe, n)
            for half in range(2):
                p0 = start_of["up", (f, half)]

                def up(i, odd):
                    def ready(k):
                        if isinstance(i, int) and i == 0 and half == 0:
                            pe.wait_ge(hn_ready, n * KD + k + 1)
                    pe_piece(pe, p0 + i, (p0 + odd) % 2, KD, 2, hn_hi, hn_lo, ready)
                steps(pe, HALF, up)
                if half == 0 and (f, 0) in ada_batch:
                    pe_flush(pe, ada_batch[f, 0])
                p1 = start_of["down", (f, half)]

                def down(i, odd):
                    def ready(k):
                        if k == 0:
                            pe.wait_ge(dve_evac, p1 - 1)
                        if k == HALF - 1:
                            pe.wait_ge(dve_evac, p1)
                    pe_piece(pe, p1 + i, (p1 + odd) % 2, HALF, 1, act_hi, act_lo, ready)
                steps(pe, KD, down)
            if (f, 1) in ada_batch:
                pe_flush(pe, ada_batch[f, 1])

        def ffn_act(act, f):
            l = f // 2
            mi = 0 if f % 2 == 0 else 6
            norm_act(act, 3 * l + 2 * (f % 2), mod[:, mi * KD:(mi + 1) * KD])
            for half in range(2):
                p0 = start_of["up", (f, half)]
                a0 = (2 * f + half) * HALF

                def up(i, odd):
                    s = (p0 + odd) % 2
                    split_act(act, *ahead(p0, HALF, WIDE, i, odd))
                    act.wait_ge(piece_done, p0 + i + 1)
                    if not (p0 == 0 and isinstance(i, int) and i < 2):
                        act.wait_ge(dve_evac, p0 + i - 1)
                    act.activation(silu[:, s], main[s][0], ACT.Silu).then_inc(act_evac, 1)
                    act.wait_ge(act_f_ready, a0 + i + 1)
                    act.activation(act_hi[:, bass.ds(i, 1), :], act_f[:, s:s + 1], ACT.Copy).then_inc(act_hi_ready, 1)
                steps(act, HALF, up)
                p1 = start_of["down", (f, half)]

                def down(i, odd):
                    s = (p1 + odd) % 2
                    split_act(act, *ahead(p1, KD, TALL, i, odd))
                    act.wait_ge(piece_done, p1 + i + 1)
                    act.wait_ge(dve_evac, p1 + i - 1)
                    act.activation(act_f[:, s], main[s][0], ACT.Copy).then_inc(act_evac, 1)
                steps(act, KD, down)

        def ffn_dve(dve, own, f):
            l = f // 2
            mi = 0 if f % 2 == 0 else 6
            norm_dve(dve, own, 3 * l + 2 * (f % 2), gains[:, l, 2 * (f % 2)], mod[:, (mi + 1) * KD:(mi + 2) * KD],
                     mod[:, mi * KD:(mi + 1) * KD])
            for half in range(2):
                p0 = start_of["up", (f, half)]
                a0 = (2 * f + half) * HALF

                def up(i, odd):
                    s = (p0 + odd) % 2
                    split_dve(dve, *ahead(p0, HALF, WIDE, i, odd))
                    dve.wait_ge(act_evac, p0 + i + 1)
                    if not (p0 == 0 and isinstance(i, int) and i < 2):
                        dve.wait_ge(dve_evac, p0 + i - 1)
                    dve.tensor_tensor(act_f[:, s], silu[:, s], main[s][1], ALU.mult).then_inc(act_f_ready, 1)
                    dve.wait_ge(act_f_ready, a0 + i + 1)
                    dve.wait_ge(act_hi_ready, a0 + i + 1)
                    dve.tensor_tensor(act_lo[:, bass.ds(i, 1), :], act_f[:, s:s + 1],
                                      act_hi[:, bass.ds(i, 1), :].bitcast(F32), ALU.subtract).then_inc(dve_evac, 1)
                steps(dve, HALF, up)
                if half == 0:
                    if (f, 0) in ada_batch:
                        dve_flush(dve, own, ada_batch[f, 0])
                    own(dve.tensor_scalar(out_gain[:], mod[:, (mi + 2) * KD:(mi + 3) * KD], 1.0, 0.5, ALU.add, ALU.mult))
                p1 = start_of["down", (f, half)]

                def down(i, odd):
                    s = (p1 + odd) % 2
                    split_dve(dve, *ahead(p1, KD, TALL, i, odd))
                    dve.wait_ge(act_evac, p1 + i + 1)
                    hj = h[:, bass.ds(i, 1), :]
                    dve.scalar_tensor_tensor(hj, act_f[:, s:s + 1], out_gain[:, bass.ds(i, 1)], hj, ALU.mult,
                                             ALU.add).then_inc(dve_evac, 1)
                steps(dve, KD, down)
            if (f, 1) in ada_batch:
                dve_flush(dve, own, ada_batch[f, 1])

        def att_scores(pe, l, u):
            n, g, U = u // 2, u % 2, 8 * l + u
            if u >= 2:
                pe.wait_ge(att_masked, U - 1)
            wide = P if n == 0 else 2 * P
            rows = slice(HD * g, HD * g + HD)
            for j in range(4):
                last = pe.matmul(ps[:, 4 + 2 * g + j // 2, (j % 2) * 256:(j % 2) * 256 + wide],
                                 proj[rows, j, n * P:(n + 1) * P], proj[rows, 4, (n + 1) * P - wide:(n + 1) * P],
                                 start=True, stop=True)
            last.then_inc(att_scored, 1)

        def project_pe(pe, kind, at, n, first_wait=None, tiles=2):
            p0 = start_of[kind, at]

            def piece(i, odd):
                def ready(k):
                    if isinstance(i, int) and i == 0 and first_wait:
                        first_wait(k)
                pe_piece(pe, p0 + i, (p0 + odd) % 2, KD, tiles, hn_hi, hn_lo, ready)
            steps(pe, n, piece)

        def unshuffle(ap, group):
            if group is None or DILATION[group] == 1:
                return ap
            return ap.rearrange("p a (r i) -> p a i r", r=DILATION[group])

        def in_order(ap, group):
            if group is None or DILATION[group] == 1:
                return ap.rearrange("p (a t) -> p a t", a=1)
            return ap.rearrange("p (a i r) -> p a i r", a=1, r=DILATION[group])

        def project_act(act, kind, at, n, size, dest, group=None):
            p0 = start_of[kind, at]

            def piece(i, odd):
                s = (p0 + odd) % 2
                split_act(act, *ahead(p0, n, size, i, odd))
                act.wait_ge(piece_done, p0 + i + 1)
                act.activation(unshuffle(dest[:, bass.ds(2 * i, 1), :], group), in_order(main[s][0], group), ACT.Copy).then_inc(act_evac, 1)
            steps(act, n, piece)

        def project_dve(dve, kind, at, n, size, dest, group=None):
            p0 = start_of[kind, at]

            def piece(i, odd):
                s = (p0 + odd) % 2
                split_dve(dve, *ahead(p0, n, size, i, odd))
                dve.wait_ge(piece_done, p0 + i + 1)
                dve.tensor_copy(unshuffle(dest[:, bass.ds(2 * i + 1, 1), :], group), in_order(main[s][1], group)).then_inc(dve_evac, 1)
            steps(dve, n, piece)

        def block_tokens(ap, group, n):
            d = DILATION[group]
            if d == 1:
                return ap[:, :, n * P:(n + 1) * P]
            if d * P == T:
                return ap.rearrange("p j (i r) -> p j r i", r=d)[:, :, n]
            k = P * d // T
            return ap.rearrange("p j (i r) -> p j r i", r=d)[:, :, k * n:k * n + k]

        def bank_tokens(ap, group):
            ap = ap.rearrange("p (j t) -> p j t", j=4)
            d = DILATION[group]
            if d == 1 or d * P == T:
                return ap
            return ap.rearrange("p j (r i) -> p j r i", r=P * d // T)

        def dsa_wide(group, n):
            return 2 * P if group == 0 and n else P

        def dsa_scores(pe, group, u):
            n, g, U = u // 2, u % 2, A0 + 8 * group + u
            if u >= 2:
                pe.wait_ge(att_masked, U - 1)
            wide = dsa_wide(group, n)
            rows = slice(HD * g, HD * g + HD)
            for j in range(4):
                last = pe.matmul(ps[:, 4 + 2 * g + j // 2, (j % 2) * 256:(j % 2) * 256 + wide],
                                 ds_qkv[rows, j, n * P:(n + 1) * P], ds_qkv[rows, 4 + j, (n + 1) * P - wide:(n + 1) * P],
                                 start=True, stop=True)
            last.then_inc(att_scored, 1)

        def second_pe(pe):
            norm_pe(pe, 3 * LAYERS)
            nn = 3 * LAYERS * KD
            project_pe(pe, "gdn_in", 0, 6, lambda k: pe.wait_ge(hn_ready, nn + k + 1))
            project_pe(pe, "gdn_ba", 0, 1, tiles=1)
            pe.wait_ge(gd_squared, 1)
            pe.wait_ge(masks_ready, 1)
            for i in range(8):
                last = pe.matmul(ps[:, i], blk[:], gd_kq[:, i // 4, i % 4], start=True, stop=True)
            last.then_inc(gd_sums, 1)
            pe.wait_ge(gd_roots, 1)
            pe.wait_ge(gd_rows_ready, 1)
            pe.wait_ge(gd_masks, 1)
            for j in range(4):
                pe.matmul(ps[:, 4 + j], sel_pair[0:8, j], gd_rows[0:8, 0], start=True, stop=True)
                last = pe.matmul(ps[:, j], sel_pair[32:40, j], gd_rows[32:40, 0], start=True, stop=True)
            last.then_inc(gd_spread, 1)
            pe.wait_ge(gd_spread_read, 1)
            for n in range(NB):
                last = pe.matmul(ps[:, 0, 8 * n:8 * n + 8], gd_rows[32:40, 0, n * P:(n + 1) * P], ident[32:40, 32:40], start=True, stop=True)
            last.then_inc(gd_log_turned, 1)
            pe.wait_ge(gd_taken_ready, 1)
            pe.wait_ge(gd_log_ready, 1)
            for j in range(4):
                for n in range(NB):
                    pe.transpose(ps[:, 4 + j, n * P:(n + 1) * P], gd_v[:, j, n * P:(n + 1) * P], ident[:])
                    last = pe.transpose(ps[:, j, n * P:(n + 1) * P], gd_kd[:, j, n * P:(n + 1) * P], ident[:])
            last.then_inc(gd_turned, 1)
            pe.wait_ge(gd_tokens_a, 1)
            pe.wait_ge(gd_tokens_b, 1)
            for g in range(2 * NB):
                j0, n = 2 * (g // NB), g % NB
                if g:
                    pe.wait_ge(delta_masked, G0 + g)
                for hp in range(2):
                    for j in range(2):
                        last = pe.matmul(ps[:, 1, (2 * hp + j) * P:(2 * hp + j + 1) * P], sel_head[32:40, 2 * (j0 + j) + hp],
                                         gd_rows[32:40, 0, n * P:(n + 1) * P], start=True, stop=True)
                last.then_inc(gd_log_spread, 1)
                delta_pe(pe, gdu, G0 + g, S0 + 2 * g + 1, n, j0, gd_kbg, gd_qd, low=(gd_kq[:, 0], gd_k), up=(gd_k, gd_kq), more=None,
                         k_tok=gd_kt, v_tok=None)
            pe.wait_ge(delta_o_ready, G0 + 2 * NB)
            pe.wait_ge(delta_state, S0 + 4 * NB + 1)
            project_pe(pe, "gdn_z", 0, 2, None)
            pe.wait_ge(gd_y_squared, 1)
            for j in range(4):
                last = pe.matmul(ps[:, 4 + j], blk[:], gd_kq[:, 0, j], start=True, stop=True)
            last.then_inc(gd_y_sums, 1)

            for group in range(3):
                if group:
                    pe.wait_ge(att_out, A0 + 8 * group)
                project_pe(pe, "dsa_in", group, 6, (lambda k: pe.wait_ge(gd_y_roots, 1)) if group == 0 else None)
                end = start_of["dsa_in", group] + 6
                pe.wait_ge(act_evac, end)
                pe.wait_ge(dve_evac, end)
                pe.wait_ge(dsa_masks, 1)
                if group:
                    pe.wait_ge(att_out, A0 + 8 * group)
                for half in range(2):
                    if half:
                        pe.wait_ge(dsa_rot_read, 2 * group + 1)
                    for j in range(4):
                        last = pe.matmul(ps[:, 4 + j], turn_half[:], ds_qkv[:, 4 * half + j], start=True, stop=True)
                    last.then_inc(dsa_rotated, 1)
                for j in range(4):
                    for n in range(NB):
                        last = pe.transpose(ps[:, j, n * P:(n + 1) * P], ds_qkv[:, 8 + j, n * P:(n + 1) * P], ident[:])
                last.then_inc(dsa_v_turned, 1)
                pe.wait_ge(dsa_v_ready, group + 1)
                pe.wait_ge(dsa_roped, 2 * group + 2)
                dsa_scores(pe, group, 0)
                for u in range(8):
                    n, g, U = u // 2, u % 2, A0 + 8 * group + u
                    nk = dsa_wide(group, n) // P
                    if u < 7:
                        dsa_scores(pe, group, u + 1)
                    pe.wait_ge(att_exp, U + 1)
                    for kt in range(nk):
                        for j in range(4):
                            last = pe.transpose(ps[:, kt, j * P:(j + 1) * P], ds_s[:, g, j, kt * P:(kt + 1) * P], ident[:])
                    last.then_inc(att_turned, 1)
                    pe.wait_ge(att_p_ready, U + 1)
                    if u >= 2:
                        pe.wait_ge(att_out, U - 1)
                    rows = slice(HD * g, HD * g + HD)
                    for j in range(4):
                        for kt in range(nk):
                            last = pe.matmul(ps[rows, 2 + g, j * P:(j + 1) * P], ds_v[:, j, n + 1 - nk + kt, rows],
                                             ds_p[:, kt, j * P:(j + 1) * P], start=(kt == 0), stop=(kt == nk - 1))
                    last.then_inc(att_pv, 1)
            project_pe(pe, "dsa_z", 0, 2, lambda k: pe.wait_ge(att_out, A0 + 24))
            end = start_of["dsa_z", 0] + 2
            pe.wait_ge(act_evac, end)
            pe.wait_ge(dve_evac, end)
            for group in range(3):
                if group:
                    pe.wait_ge(dsa_rows, group)
                for which in range(2):
                    for n in range(NB):
                        last = pe.matmul(ps[0:8, which, n * P:(n + 1) * P], ds_stat[:, group, which, n], ident[:], start=True, stop=True)
                last.then_inc(dsa_stat_turned, 1)
            for group in range(3):
                pe.wait_ge(dsa_weights, 1)
                if group:
                    pe.wait_ge(dsa_mixed, group)
                for j in range(4):
                    last = pe.matmul(ps[:, 4 + j], sel_mix[0:8, j], ds_rows[0:8, group], start=True, stop=True)
                last.then_inc(dsa_weights_spread, 1)

            def merge(i, odd, p0, y_hi, y_lo):
                p, slot = p0 + i, (p0 + odd) % 2
                pe.wait_ge(w_lo_ready, p + 1)
                pe.wait_ge(act_evac, p - 1)
                pe.wait_ge(dve_evac, p - 1)
                for k in range(KD + 4):
                    x_hi, x_lo, t = (hn_hi, hn_lo, 0) if k < KD else (y_hi, y_lo, 1)
                    kk, n = (k, KD) if k < KD else (k - KD, 4)
                    wh, wl = w_hi[:, slot, k * P:(k + 1) * P], w_lo[:, slot, k * P:(k + 1) * P]
                    pe.matmul(main[slot][t], wh, x_hi[:, kk], start=(kk == 0), stop=False)
                    pe.matmul(main[slot][t], wh, x_lo[:, kk], start=False, stop=False)
                    last = pe.matmul(main[slot][t], wl, x_hi[:, kk], start=False, stop=(kk == n - 1))
                last.then_inc(piece_done, 1)
            pe.wait_ge(ya_ready, 1)
            steps(pe, KD, lambda i, odd: merge(i, odd, start_of["merge", 0], ya_hi, ya_lo))
            steps(pe, KD, lambda i, odd: merge(i, odd, start_of["merge", 1], yb_hi, yb_lo))
            project_pe(pe, "last", 0, 4, lambda k: pe.wait_ge(merged, 1))
            norm_pe(pe, 3 * LAYERS + 1)

        def second_act(act):
            act.wait_ge(vec2_loaded, 16)
            act.wait_ge(dve_evac, start_of["gdn_in", 0])
            norm_act(act, 3 * LAYERS, None)
            project_act(act, "gdn_in", 0, 6, WIDE, gd_raw)
            p = start_of["gdn_ba", 0]
            split_act(act, (p + 1, (p + 1) % 2), WIDE)
            act.wait_ge(piece_done, p + 1)
            s = p % 2
            act.activation(gd_rows[0:8, 0], ps[0:8, 2 * s], ACT.Sigmoid)
            act.activation(gd_rows[32:40, 1], ps[32:40, 2 * s], ACT.Abs, bias=v2("dt")[32:40])
            act.activation(gd_rows[32:40, 2], ps[32:40, 2 * s], ACT.Relu, bias=v2("dt")[32:40]).then_inc(act_evac, 1)
            act.wait_ge(act_evac, p + 1)
            act.activation(gd_rows[32:40, 1], gd_rows[32:40, 1], ACT.Exp, scale=-1.0).then_inc(act_own, 1)
            act.wait_ge(act_own, 1)
            act.activation(gd_rate[32:40], v2("a_log")[32:40], ACT.Exp)
            act.activation(gd_rows[32:40, 1], gd_rows[32:40, 1], ACT.Ln, bias=ones[32:40, 0:1]).then_inc(gd_softplus, 1)
            act.wait_ge(gd_conv, 4 * 6)
            act.activation(gd_q[:], gd_q[:], ACT.Silu)
            act.activation(gd_k[:], gd_k[:], ACT.Silu)
            act.activation(gd_v[:], gd_v[:], ACT.Silu).then_inc(act_own, 1)
            act.wait_ge(act_own, 2)
            act.activation(gd_kq[:, 0], gd_q[:], ACT.Square)
            act.activation(gd_kq[:, 1], gd_k[:], ACT.Square).then_inc(gd_squared, 1)
            act.wait_ge(gd_sums, 1)
            act.activation(gd_kq[:].rearrange("p a j t -> p (a j) t"), ps[:, 0:8], ACT.Sqrt, bias=eps[:]).then_inc(gd_roots, 1)
            act.wait_ge(gd_spread, 1)
            act.wait_ge(gd_normed, 1)
            act.activation(gd_kd[:], ps[:, 0:4], ACT.Copy)
            act.activation(gd_qd[:], ps[:, 0:4], ACT.Exp).then_inc(gd_exp_log, 1)
            act.wait_ge(gd_to_end, 1)
            act.activation(gd_kd[:], gd_kd[:], ACT.Exp).then_inc(gd_exp_to_end, 1)
            act.wait_ge(gd_log_turned, 1)
            act.activation(gd_neglog[:].rearrange("p n h -> p (n h)"), ps[:, 0, 0:8 * NB], ACT.Copy, scale=-1.0).then_inc(gd_log_ready, 1)
            act.wait_ge(gd_turned, 1)
            act.activation(gd_vt[:].rearrange("p a b c -> p a (b c)"), ps[:, 4:8], ACT.Copy).then_inc(gd_tokens_a, 1)
            for g in range(2 * NB):
                j0, n = 2 * (g // NB), g % NB
                act.wait_ge(gd_log_spread, g + 1)
                if g:
                    act.wait_ge(delta_masked, G0 + g)
                else:
                    act.wait_ge(gd_log_ready, 1)
                    act.wait_ge(gd_turned, 1)
                for hp in range(2):
                    for j in range(2):
                        hd = 2 * (j0 + j) + hp
                        last = act.activation(gd_e[:, hp, j], ps[:, 1, (2 * hp + j) * P:(2 * hp + j + 1) * P], ACT.Abs,
                                              bias=gd_neglog[:, n, hd:hd + 1])
                last.then_inc(act_own, 1)
                act.wait_ge(act_own, 3 + g)
                act.activation(gd_e[:], gd_e[:], ACT.Exp, scale=-1.0).then_inc(gd_e_ready, 1)
                delta_act(act, gdu, G0 + g, n, gd_y[:, j0:j0 + 2, n * P:(n + 1) * P], False)
            act.wait_ge(delta_state, S0 + 4 * NB + 1)
            project_act(act, "gdn_z", 0, 2, WIDE, gd_z)
            end = start_of["gdn_z", 0] + 2
            act.wait_ge(delta_o_ready, G0 + 2 * NB)
            act.wait_ge(act_evac, end)
            act.wait_ge(dve_evac, end)
            act.activation(gd_z[:], gd_z[:], ACT.Silu)
            act.activation(gd_kq[:, 0], gd_y[:], ACT.Square).then_inc(gd_y_squared, 1)
            act.wait_ge(gd_y_sums, 1)
            act.activation(gd_kq[:, 1], ps[:, 4:8], ACT.Sqrt, bias=eps[:], scale=1.0 / HD).then_inc(gd_y_roots, 1)
            act.wait_ge(gd_y_ready, 1)
            act.activation(yb_hi[:], gd_y[:], ACT.Copy).then_inc(yb_high, 1)
            act.wait_ge(yb_ready, 1)
            for group in range(3):
                if group:
                    act.wait_ge(att_out, A0 + 8 * group)
                project_act(act, "dsa_in", group, 6, WIDE, ds_qkv, group)
                act.wait_ge(dsa_v_turned, group + 1)
                act.activation(ds_v[:].rearrange("p a b c -> p a (b c)"), ps[:, 0:4], ACT.Copy).then_inc(dsa_v_ready, 1)

                def exps(u):
                    U, g = A0 + 8 * group + u, u % 2
                    n = u // 2
                    wide = dsa_wide(group, n)
                    act.wait_ge(att_max, U + 1)
                    for j in range(4):
                        last = act.activation(ds_s[:, g, j, 0:wide], ds_s[:, g, j, 0:wide], ACT.Exp, bias=att_nm[:, g, j:j + 1],
                                              accum_out=ds_stat[:, group, 1, n, 4 * g + j:4 * g + j + 1])
                    last.then_inc(att_exp, 1)
                exps(0)
                for u in range(8):
                    n, g, U = u // 2, u % 2, A0 + 8 * group + u
                    nk = dsa_wide(group, n) // P
                    if u < 7:
                        exps(u + 1)
                    act.wait_ge(att_turned, U + 1)
                    if U:
                        act.wait_ge(att_pv, U)
                    act.activation(ds_p[:, 0:nk], ps[:, 0:nk], ACT.Copy).then_inc(att_p_ready, 1)
                    act.wait_ge(att_pv, U + 1)
                    rows = slice(HD * g, HD * g + HD)
                    for j in range(4):
                        last = act.activation(block_tokens(ds_o[group][rows, j:j + 1], group, n),
                                              bank_tokens1(ps[rows, 2 + g, j * P:(j + 1) * P], group), ACT.Copy)
                    last.then_inc(att_out, 1)
            project_act(act, "dsa_z", 0, 2, WIDE, ds_z)
            end = start_of["dsa_z", 0] + 2
            act.wait_ge(dve_evac, end)
            act.wait_ge(act_evac, end)
            act.activation(ds_z[:], ds_z[:], ACT.Silu).then_inc(dsa_z_ready, 1)
            act.wait_ge(dsa_shifted, 1)
            act.activation(ds_rows[0:8, 0:3], ds_rows[0:8, 0:3], ACT.Exp).then_inc(dsa_exp_shifted, 1)
            act.wait_ge(ya_f_ready, 1)
            act.activation(ya_hi[:], ds_o[0][:], ACT.Copy).then_inc(ya_high, 1)
            for part in range(2):
                p0 = start_of["merge", part]

                def piece(i, odd):
                    s = (p0 + odd) % 2
                    split_act(act, *ahead(p0, KD, MERGE, i, odd))
                    act.wait_ge(piece_done, p0 + i + 1)
                    act.wait_ge(dve_evac, p0 + i - 1)
                    if part == 0 and isinstance(i, int) and i == 0:
                        act.wait_ge(ya_ready, 1)
                    act.activation(mg_g[:, s], main[s][0], ACT.Sigmoid).then_inc(act_evac, 1)
                steps(act, KD, piece)
            act.wait_ge(dve_evac, start_of["merge", 1] + KD)
            act.activation(hn_hi[:], mg[:], ACT.Copy).then_inc(merged_hi, 1)
            p0 = start_of["last", 0]

            def piece(i, odd):
                s = (p0 + odd) % 2
                split_act(act, *ahead(p0, 4, WIDE, i, odd))
                act.wait_ge(piece_done, p0 + i + 1)
                act.wait_ge(dve_evac, p0 + i - 1)
                act.activation(tmp[:, s], main[s][0], ACT.Copy).then_inc(act_evac, 1)
            steps(act, 4, piece)
            act.wait_ge(dve_evac, p0 + 4)
            norm_act(act, 3 * LAYERS + 1, None, last=True)

        def second_dve(dve, own):
            dve.wait_ge(vec2_loaded, 16)
            dve.wait_ge(masks_ready, 1)
            norm_dve(dve, own, 3 * LAYERS, v2("norm", 0, 8), None, None)
            p0 = start_of["gdn_in", 0]

            def piece(i, odd):
                s = (p0 + odd) % 2
                split_dve(dve, *ahead(p0, 6, WIDE, i, odd))
                dve.wait_ge(piece_done, p0 + i + 1)
                dve.tensor_copy(gd_raw[:, bass.ds(2 * i + 1, 1), :], in_order(main[s][1], None)).then_inc(dve_evac, 1)
                dve.wait_ge(act_evac, p0 + i + 1)
                dve.wait_ge(dve_evac, p0 + i + 1)
                for back in range(4):
                    for t in range(2):
                        c = gd_conv_out[:, bass.ds(2 * i + t, 1), back:T]
                        raw = gd_raw[:, bass.ds(2 * i + t, 1), 0:T - back]
                        tap = vec2[:, bass.ds(2 * i + (VEC2_AT["conv"] + 12 * (3 - back) + t), 1)]
                        if back == 0:
                            last = dve.tensor_scalar(c, raw, tap, None, ALU.mult)
                        else:
                            last = dve.scalar_tensor_tensor(c, raw, tap, c, ALU.mult, ALU.add)
                    last.then_inc(gd_conv, 1)
                    if back < 3:
                        dve.wait_ge(gd_conv, 4 * i + back + 1)
            steps(dve, 6, piece)
            end = start_of["gdn_ba", 0]
            split_dve(dve, (end + 1, (end + 1) % 2), WIDE)
            dve.wait_ge(act_evac, end + 1)
            dve.tensor_copy(out_gain[:], norm_gain[:]).then_inc(dve_evac, 1)
            dve.wait_ge(dve_evac, end + 1)
            dve.wait_ge(gd_conv, 4 * 6)
            dve.wait_ge(gd_softplus, 1)
            g_rows = gd_rows[32:40]
            own(dve.tensor_tensor(g_rows[:, 1], g_rows[:, 1], g_rows[:, 2], ALU.add))
            own(dve.tensor_scalar(g_rows[:, 1], g_rows[:, 1], gd_rate[32:40], -1.0, ALU.mult, ALU.mult))
            dve.tensor_tensor_scan(g_rows[:, 0], restart[32:40], g_rows[:, 1], 0.0, ALU.mult, ALU.add).then_inc(gd_rows_ready, 1)
            dve.wait_ge(gd_roots, 1)
            own(dve.reciprocal(gd_kq[:], gd_kq[:]))
            own(dve.tensor_tensor(gd_k[:], gd_k[:], gd_kq[:, 1], ALU.mult))
            own(dve.scalar_tensor_tensor(gd_kq[:, 1], gd_q[:], HD ** -0.5, gd_kq[:, 0], ALU.mult, ALU.mult))
            dve.wait_ge(gd_spread, 1)
            own(dve.tensor_tensor(gd_kq[:, 0], gd_k[:], ps[:, 4:8], ALU.mult))
            dve.tensor_tensor(gd_v[:], gd_v[:], ps[:, 4:8], ALU.mult).then_inc(gd_normed, 1)
            dve.wait_ge(gd_exp_log, 1)
            ends = gd_kd[:].rearrange("p j (c i) -> p (j c) i", i=HD)
            own(dve.tensor_copy(gd_decay[:], gd_qd[:].rearrange("p j (c i) -> p j c i", i=HD)[:, :, :, HD - 1]))
            dve.tensor_copy(gd_ends[:], ends[:, :, HD - 1]).then_inc(gd_spread_read, 1)
            dve.wait_ge(gd_spread_read, 1)
            dve.tensor_tensor(ends, gd_ends[:].unsqueeze(2).broadcast_to([P, 32, HD]), ends, ALU.subtract).then_inc(gd_to_end, 1)
            own(dve.tensor_tensor(gd_kbg[:], gd_kq[:, 0], gd_qd[:], ALU.mult))
            own(dve.tensor_tensor(gd_qd[:], gd_kq[:, 1], gd_qd[:], ALU.mult))
            dve.wait_ge(gd_exp_to_end, 1)
            dve.tensor_tensor(gd_kd[:], gd_k[:], gd_kd[:], ALU.mult).then_inc(gd_taken_ready, 1)
            dve.wait_ge(gd_turned, 1)
            dve.tensor_copy(gd_kt[:].rearrange("p a b c -> p a (b c)"), ps[:, 0:4]).then_inc(gd_tokens_b, 1)
            own(dve.memset(state_p[:], 0.0))
            dve.memset(state[:], 0.0).then_inc(delta_state, 1)

            def mask_products(g):
                dve.wait_ge(gd_e_ready, g + 1)
                for hp in range(2):
                    low = ps[:, 4 + hp, 0:256].rearrange("p (j t) -> p j t", j=2)
                    dve.tensor_tensor(gdu.x[:, hp], low, pair_low[:].unsqueeze(1).broadcast_to([P, 2, P]), ALU.mult)
                    both = up_mask[:].unsqueeze(1).broadcast_to([P, 2, 2, P])
                    last = dve.tensor_tensor(gdu.mb[:, hp], ps[:, 6 + hp].rearrange("p (j w t) -> p j w t", j=2, w=2), both, ALU.mult)
                own(last)
                own(dve.tensor_tensor(gdu.x[:], gdu.x[:], gd_e[:], ALU.mult))
                mb = gdu.mb[:].rearrange("p h j w t -> p (h j) w t")
                own(dve.tensor_tensor(mb, mb, gd_e[:].rearrange("p h j t -> p (h j) t").unsqueeze(2).broadcast_to([P, 4, 2, P]), ALU.mult))
            for g in range(2 * NB):
                j0, n = 2 * (g // NB), g % NB
                if g == 0:
                    dve.wait_ge(gd_tokens_a, 1)
                delta_dve(dve, own, gdu, G0 + g, n, S0 + 2 * g + 1, lambda c: gd_decay[:, j0:j0 + 2, c:c + 1], lambda: mask_products(g),
                          j0=j0, w=gd_vt[:, j0:j0 + 2, n])
            dve.wait_ge(delta_o_ready, G0 + 2 * NB)
            project_dve(dve, "gdn_z", 0, 2, WIDE, gd_z)
            dve.wait_ge(gd_y_roots, 1)
            own(dve.reciprocal(gd_kq[:, 1], gd_kq[:, 1]))
            own(dve.scalar_tensor_tensor(gd_y[:], gd_y[:], v2("gdn_norm"), gd_kq[:, 1], ALU.mult, ALU.mult))
            dve.tensor_tensor(gd_y[:], gd_y[:], gd_z[:], ALU.mult).then_inc(gd_y_ready, 1)
            dve.wait_ge(yb_high, 1)
            dve.tensor_tensor(yb_lo[:], gd_y[:], yb_hi[:].bitcast(F32), ALU.subtract).then_inc(yb_ready, 1)

            dve.wait_ge(yb_ready, 1)
            for group in range(3):
                if group:
                    dve.wait_ge(att_pv, A0 + 8 * group)
                project_dve(dve, "dsa_in", group, 6, WIDE, ds_qkv, group)
                dve.wait_ge(dsa_tables, 16 * (group + 1))
                for half in range(2):
                    n = 2 * group + half
                    x = ds_qkv[:, 4 * half:4 * half + 4]
                    bc = lambda t: ds_table[:, t:t + 1].broadcast_to([P, 4, T])
                    dve.wait_ge(dsa_rotated, n + 1)
                    own(dve.tensor_tensor(x, x, bc(0), ALU.mult))
                    dve.tensor_tensor(ds_t[:], ps[:, 4:8], bc(1), ALU.mult).then_inc(dsa_rot_read, 1)
                    dve.wait_ge(dsa_rot_read, n + 1)
                    dve.tensor_tensor(x, x, ds_t[:], ALU.add).then_inc(dsa_roped, 1)
                    dve.wait_ge(dsa_roped, n + 1)

                def masked(u):
                    U, g = A0 + 8 * group + u, u % 2
                    n = u // 2
                    wide = dsa_wide(group, n)
                    dve.wait_ge(att_scored, U + 1)
                    if U >= 2:
                        dve.wait_ge(att_turned, U - 1)
                    s = ds_s[:, g, :, 0:wide]
                    scores = ps[:, 4 + 2 * g:6 + 2 * g].rearrange("p b (j k) -> p (b j) k", k=256)[:, :, 0:wide]
                    m = ds_mask[:, 2 * P:3 * P] if group == 2 else ds_mask[:, 2 * P - wide:2 * P]
                    dve.scalar_tensor_tensor(s, scores, HD ** -0.5, m.unsqueeze(1).broadcast_to([P, 4, wide]),
                                             ALU.mult, ALU.add).then_inc(att_masked, 1)
                    dve.wait_ge(att_masked, U + 1)
                    mx = ds_stat[:, group, 0, n, 4 * g:4 * g + 4]
                    own(dve.tensor_reduce(mx, s, AX.X, ALU.max))
                    dve.tensor_scalar(att_nm[:, g], mx, -1.0, None, ALU.mult).then_inc(att_max, 1)
                for u in range(8):
                    masked(u)
            dve.wait_ge(att_out, A0 + 24)
            project_dve(dve, "dsa_z", 0, 2, WIDE, ds_z)
            for group in range(3):
                dve.wait_ge(dsa_stat_turned, group + 1)
                for which in range(2):
                    row = ds_rows[0:8, 3 * which + group:3 * which + group + 1]
                    last = dve.tensor_copy(rows_order(row, group), bank_order(ps[0:8, which], group))
                last.then_inc(dsa_rows, 1)
            dve.wait_ge(dsa_rows, 3)
            r = ds_rows[0:8]
            own(dve.tensor_tensor(r[:, 6], r[:, 0], r[:, 1], ALU.max))
            own(dve.tensor_tensor(r[:, 6], r[:, 6], r[:, 2], ALU.max))
            dve.tensor_tensor(r[:, 0:3], r[:, 0:3], r[:, 6:7].broadcast_to([8, 3, T]), ALU.subtract).then_inc(dsa_shifted, 1)
            dve.wait_ge(dsa_exp_shifted, 1)
            own(dve.tensor_tensor(r[:, 3:6], r[:, 3:6], r[:, 0:3], ALU.mult))
            own(dve.tensor_tensor(r[:, 6], r[:, 3], r[:, 4], ALU.add))
            own(dve.tensor_tensor(r[:, 6], r[:, 6], r[:, 5], ALU.add))
            own(dve.reciprocal(r[:, 6], r[:, 6]))
            dve.tensor_tensor(r[:, 0:3], r[:, 0:3], r[:, 6:7].broadcast_to([8, 3, T]), ALU.mult).then_inc(dsa_weights, 1)
            for group in range(3):
                dve.wait_ge(dsa_weights_spread, group + 1)
                dve.tensor_tensor(ds_o[group][:], ds_o[group][:], ps[:, 4:8], ALU.mult).then_inc(dsa_mixed, 1)
            dve.wait_ge(dsa_mixed, 3)
            own(dve.tensor_tensor(ds_o[0][:], ds_o[0][:], ds_o[1][:], ALU.add))
            own(dve.tensor_tensor(ds_o[0][:], ds_o[0][:], ds_o[2][:], ALU.add))
            dve.wait_ge(dsa_z_ready, 1)
            dve.tensor_tensor(ds_o[0][:], ds_o[0][:], ds_z[:], ALU.mult).then_inc(ya_f_ready, 1)
            dve.wait_ge(ya_high, 1)
            dve.tensor_tensor(ya_lo[:], ds_o[0][:], ya_hi[:].bitcast(F32), ALU.subtract).then_inc(ya_ready, 1)
            for part in range(2):
                p0 = start_of["merge", part]
                if part:
                    dve.wait_ge(dve_evac, p0)

                def piece(i, odd):
                    s = (p0 + odd) % 2
                    split_dve(dve, *ahead(p0, KD, MERGE, i, odd))
                    dve.wait_ge(act_evac, p0 + i + 1)
                    mj = mg[:, bass.ds(i, 1), :].rearrange("p a t -> p (a t)")
                    if part == 0:
                        dve.tensor_tensor(mj, mg_g[:, s], main[s][1], ALU.mult).then_inc(dve_evac, 1)
                    else:
                        dve.tensor_tensor(mg_g[:, s], mg_g[:, s], main[s][1], ALU.mult).then_inc(mg_step, 1)
                        dve.wait_ge(mg_step, i + 1)
                        dve.tensor_tensor(mj, mj, mg_g[:, s], ALU.add).then_inc(dve_evac, 1)
                steps(dve, KD, piece)
            dve.wait_ge(merged_hi, 1)
            dve.tensor_tensor(hn_lo[:], mg[:], hn_hi[:].bitcast(F32), ALU.subtract).then_inc(merged, 1)
            p0 = start_of["last", 0]

            def piece(i, odd):
                s = (p0 + odd) % 2
                split_dve(dve, *ahead(p0, 4, WIDE, i, odd))
                dve.wait_ge(act_evac, p0 + i + 1)
                for t in range(2):
                    hj = h[:, bass.ds(2 * i + t, 1), :].rearrange("p a t -> p (a t)")
                    last = dve.tensor_tensor(hj, hj, tmp[:, s] if t == 0 else main[s][1], ALU.add)
                last.then_inc(dve_evac, 1)
            steps(dve, 4, piece)
            dve.wait_ge(norm_sqrt, 3 * LAYERS + 2)
            own(dve.reciprocal(rstd[:], rstd[:]))
            for j in range(KD):
                last = dve.scalar_tensor_tensor(mg[:, j], h[:, j], v2("final", j), rstd[:], ALU.mult, ALU.mult)
            last.then_inc(h_final, 1)

        def rows_order(row, group):
            if DILATION[group] == 1:
                return row
            return row.rearrange("p a (i r) -> p a r i", r=DILATION[group])

        def bank_order(ap, group):
            if DILATION[group] == 1:
                return ap.rearrange("p (a t) -> p a t", a=1)
            return ap.rearrange("p (a r i) -> p a r i", a=1, r=DILATION[group])

        def bank_tokens1(ap, group):
            d = DILATION[group]
            ap = ap.rearrange("p (j t) -> p j t", j=1)
            if d == 1 or d * P == T:
                return ap
            return ap.rearrange("p j (r i) -> p j r i", r=P * d // T)

        def mix_pe(pe, l):
            v = l + 1
            norm_pe(pe, 3 * l + 1)
            p0 = start_of["mix_in", (l, 0)]

            def piece(i, odd):
                def ready(k):
                    if isinstance(i, int) and i == 0:
                        pe.wait_ge(hn_ready, (3 * l + 1) * KD + k + 1)
                pe_piece(pe, p0 + i, (p0 + odd) % 2, KD, 2, hn_hi, hn_lo, ready)
            steps(pe, MIX_TILES // 2, piece)

            pe.wait_ge(qk_squared, v)
            if l == 0:
                pe.wait_ge(masks_ready, 1)
            for i in range(5):
                last = pe.matmul(ps[:, (4, 5, 6, 7, 0)[i]], blk[:], att_r[:, i], start=True, stop=True)
            last.then_inc(qk_sums, 1)
            pe.wait_ge(qk_roots, v)
            for n in range(NB):
                last = pe.transpose(ps[:, 4, n * P:(n + 1) * P], proj[:, 5, n * P:(n + 1) * P], ident[:])
            last.then_inc(att_v_turned, 1)
            pe.wait_ge(att_v_ready, v)
            pe.wait_ge(qk_normed, v)
            att_scores(pe, l, 0)
            for u in range(8):
                n, g, U = u // 2, u % 2, 8 * l + u
                nk = 1 if n == 0 else 2
                if u < 7:
                    att_scores(pe, l, u + 1)
                pe.wait_ge(att_probs, U + 1)
                for kt in range(nk):
                    for j in range(4):
                        last = pe.transpose(ps[:, kt, j * P:(j + 1) * P], att_s[:, g, j, kt * P:(kt + 1) * P], ident[:])
                last.then_inc(att_turned, 1)
                pe.wait_ge(att_p_ready, U + 1)
                if u >= 2:
                    pe.wait_ge(att_out, U - 1)
                rows = slice(HD * g, HD * g + HD)
                for kt in range(nk):
                    last = pe.matmul(ps[rows, 2 + g], att_v[:, n + 1 - nk + kt, rows], att_p[:, kt], start=(kt == 0),
                                     stop=(kt == nk - 1))
                last.then_inc(att_pv, 1)

            pe.wait_ge(lora_ready, v)
            pe.wait_ge(att_out, 8 * v)
            pe.wait_ge(lora_loaded, 16 * v)
            for j in range(2):
                cols = slice(j * P, (j + 1) * P)
                pe.matmul(ps[:, 4 + j], lora[0:HD, 0, cols], proj[0:HD, 12], start=True, stop=True)
                pe.matmul(ps[:, 6 + j], lora[HD:P, 0, cols], proj[HD:P, 12], start=True, stop=True)
                last = pe.matmul(ps[:, j], lora[:, 1, cols], proj[:, 13], start=True, stop=True)
            last.then_inc(lora_out, 1)
            pe.wait_ge(kk_squared, v)
            pe.wait_ge(gates_ready, v)
            for j in range(2):
                last = pe.matmul(ps[:, 4 + j], blk[:], rw_bonus[:, j], start=True, stop=True)
            last.then_inc(kk_sums, 1)
            pe.wait_ge(bonus_raw, v)
            for j in range(2):
                last = pe.matmul(ps[:, 6 + j], blk[:], rw_bonus[:, j], start=True, stop=True)
            last.then_inc(bonus_sums, 1)
            pe.wait_ge(factors_ready, v)
            for i, src in enumerate((proj[:, 10], proj[:, 11], rw_a[:, 0], rw_a[:, 1], rw_ed[:, 0], rw_ed[:, 1])):
                for n in range(NB):
                    last = pe.transpose(ps[:, (4, 5, 6, 7, 0, 1)[i], n * P:(n + 1) * P], src[:, n * P:(n + 1) * P], ident[:])
            last.then_inc(rw_turned, 1)
            pe.wait_ge(rw_tokens_a, v)
            pe.wait_ge(rw_tokens_b, v)
            for n in range(NB):
                blk_t = slice(n * P, (n + 1) * P)
                delta_pe(pe, rwu, l * NB + n, 9 * l + 1 + 2 * n, n, 0, rw_kr[:, 0], rw_kr[:, 1],
                         low=(rw_kr[:, 0], rw_bi), up=(rw_bi, rw_kr), more=(rw_ki, rw_kr), k_tok=rw_bt, v_tok=(rw_kt, rw_vt))
            pe.wait_ge(delta_o_ready, NB * v)
            for j in range(2):
                last = pe.matmul(ps[:, 4 + j], blk[:], rw_y[:, j], start=True, stop=True)
            last.then_inc(gn_sums, 1)
            pe.wait_ge(gn_squared, v)
            for j in range(2):
                last = pe.matmul(ps[:, 6 + j], blk[:], rw_r[:, j], start=True, stop=True)
            last.then_inc(gn_square_sums, 1)

            p1 = start_of["mix_out", (l, 0)]

            def out_piece(i, odd):
                def ready(k):
                    if isinstance(i, int) and i == 0 and k == 0:
                        pe.wait_ge(mixed_ready, v)
                pe_piece(pe, p1 + i, (p1 + odd) % 2, KD, 2, hn_hi, hn_lo, ready)
            steps(pe, KD // 2, out_piece)

        def delta_pe(pe, d, g, h_count, n, j0, key_q, read_q, low, up, more, k_tok, v_tok):
            t = slice(n * P, (n + 1) * P)
            if g:
                pe.wait_ge(delta_o_ready, g)
            pe.wait_ge(delta_state, h_count)
            for hp in range(2):
                rows = slice(HD * hp, HD * hp + HD)
                for j in range(2):
                    pe.matmul(ps[:, 4 + hp, j * P:(j + 1) * P], low[0][rows, j0 + j, t], low[1][rows, j0 + j, t], start=True, stop=True)
                    last = pe.matmul(ps[:, 6 + hp, j * 256:(j + 1) * 256], up[0][rows, j0 + j, t], up[1][rows, :, j0 + j, t],
                                     start=True, stop=True)
                    if more:
                        last = pe.matmul(ps[:, hp, j * 256:(j + 1) * 256], more[0][rows, j0 + j, t], more[1][rows, :, j0 + j, t],
                                         start=True, stop=True)
            last.then_inc(delta_mats, 1)
            pe.wait_ge(delta_masked, g + 1)
            if more:
                for j in range(2):
                    for hp in range(2):
                        last = pe.matmul(ps[:, 1, j * P + hp * HD:j * P + hp * HD + HD], d.mc[:, hp, j, 0],
                                         v_tok[1][:, j0 + j, n, hp * HD:hp * HD + HD], start=True, stop=True)
                last.then_inc(delta_w1_summed, 1)
            for m, lv in enumerate(LEVELS):
                i = len(LEVELS) * g + m
                pe.wait_ge(delta_bt_ready, i + 1)
                for hp in range(2):
                    if m:
                        pe.wait_ge(delta_x_ready, 2 * (i - g - 1) + hp + 1)
                    for j in range(2):
                        last = pe.matmul(ps[:, V1_BANK[hp], j * P:(j + 1) * P], d.bt[:, m % 2, hp, j], d.x[:, hp, j], start=True, stop=True)
                    last.then_inc(delta_v1_summed, 1)
                for hp in range(2):
                    if m:
                        pe.wait_ge(delta_y_ready, 2 * (i - 1) + hp + 1)
                    pe.wait_ge(delta_v1_ready, 2 * i + hp + 1)
                    for j in range(2):
                        c = slice(j * P, (j + 1) * P)
                        if m < len(LEVELS) - 1:
                            pe.matmul(ps[:, X_BANK[hp], c], d.y[:, hp, j], d.v1[:, hp, j], start=True, stop=True)
                        last = pe.matmul(ps[:, Y_BANK[hp], c], d.v1[:, hp, j], d.y[:, hp, j], start=True, stop=True)
                    last.then_inc(delta_xy_summed, 1)
            pe.wait_ge(delta_y_ready, 2 * len(LEVELS) * (g + 1))
            for c in range(2):
                C = 2 * g + c
                tc = slice(HD * c, HD * c + HD)
                tok = slice(n * P + HD * c, n * P + HD * c + HD)
                pe.wait_ge(delta_state, h_count + c)
                for j in range(2):
                    last = pe.matmul(ps[tc, 6, j * P:(j + 1) * P], key_q[:, j0 + j, tok], state[:, j0 + j], start=True, stop=True)
                last.then_inc(delta_q_summed, 1)
                for j in range(2):
                    pe.matmul(ps[:, 3, j * P + HD * c:j * P + HD * c + HD], state[:, j0 + j], read_q[:, j0 + j, tok],
                              start=(c == 0 and j == 0), stop=False, skip_group_check=True)
                pe.wait_ge(delta_rhs_ready, C + 1)
                for j in range(2):
                    for hp in range(2):
                        col = slice(j * P + hp * HD, j * P + hp * HD + HD)
                        last = pe.matmul(ps[tc, 7, col], d.y[tc, hp, j, tc], d.rhs[tc, j, hp * HD:hp * HD + HD], start=True, stop=True)
                last.then_inc(delta_u_summed, 1)
                pe.wait_ge(delta_u_ready, C + 1)
                for j in range(2):
                    last = pe.matmul(ps[:, 0, j * P:(j + 1) * P], k_tok[tc, j0 + j, n], d.u[tc, j], start=True, stop=not v_tok)
                    if v_tok:
                        last = pe.matmul(ps[:, 0, j * P:(j + 1) * P], v_tok[0][tc, j0 + j, n], v_tok[1][tc, j0 + j, n],
                                         start=False, stop=True)
                last.then_inc(delta_s_summed, 1)
            for j in range(2):
                for hp in range(2):
                    rows = slice(HD * hp, HD * hp + HD)
                    bank = ps[rows, 3, j * P:(j + 1) * P]
                    last = pe.matmul(bank, d.u[:, j, rows], d.mb[:, hp, j, 1], start=False, stop=not v_tok, skip_group_check=True)
                    if v_tok:
                        last = pe.matmul(bank, v_tok[1][:, j0 + j, n, rows], d.mc[:, hp, j, 1], start=False, stop=True,
                                         skip_group_check=True)
            last.then_inc(delta_o_summed, 1)

        def delta_act(act, d, g, n, out_, more):
            if more:
                act.wait_ge(delta_w1_summed, g + 1)
                act.activation(d.w1[:].rearrange("p a b -> p (a b)"), ps[:, 1, 0:256], ACT.Copy, scale=-1.0).then_inc(delta_w1_ready, 1)
            for m in range(len(LEVELS)):
                i = len(LEVELS) * g + m
                for hp in range(2):
                    act.wait_ge(delta_v1_summed, 2 * i + hp + 1)
                    act.activation(d.v1[:, hp].rearrange("p a b -> p (a b)"), ps[:, V1_BANK[hp], 0:2 * P], ACT.Copy).then_inc(delta_v1_ready, 1)
            act.wait_ge(delta_o_summed, g + 1)
            act.activation(out_, ps[:, 3, 0:256].rearrange("p (j t) -> p j t", j=2), ACT.Copy).then_inc(delta_o_ready, 1)

        def delta_dve(dve, own, d, g, n, h_count, decay, mask_pair, j0=0, w=None):
            dve.wait_ge(delta_mats, g + 1)
            if g:
                dve.wait_ge(delta_o_summed, g)
            mask_pair()
            ident4 = ident[:].unsqueeze(1).unsqueeze(1).broadcast_to([P, 2, 2, P])
            own(dve.tensor_tensor(d.y[:], d.mb[:, :, :, 0], level[:, 0].unsqueeze(1).unsqueeze(1).broadcast_to([P, 2, 2, P]), ALU.mult))
            own(dve.tensor_tensor(d.y[:], ident4, d.y[:], ALU.subtract))
            dve.tensor_tensor(d.x[:], ident4, d.x[:], ALU.subtract).then_inc(delta_masked, 1)
            for m in range(len(LEVELS)):
                i = len(LEVELS) * g + m
                for hp in range(2):
                    dve.wait_ge(delta_xy_summed, 2 * i + hp + 1)
                    yf = d.y[:, hp].rearrange("p a b -> p (a b)")
                    xf = d.x[:, hp].rearrange("p a b -> p (a b)")
                    if m < len(LEVELS) - 1:
                        dve.tensor_tensor(xf, xf, ps[:, X_BANK[hp], 0:2 * P], ALU.subtract).then_inc(delta_x_ready, 1)
                    dve.tensor_tensor(yf, yf, ps[:, Y_BANK[hp], 0:2 * P], ALU.subtract).then_inc(delta_y_ready, 1)
            if w is None:
                dve.wait_ge(delta_w1_ready, g + 1)
                w = d.w1
            hs = slice(j0, j0 + 2)
            dve.wait_ge(delta_y_ready, 2 * len(LEVELS) * (g + 1))
            for c in range(2):
                C = 2 * g + c
                tc = slice(HD * c, HD * c + HD)
                dve.wait_ge(delta_q_summed, C + 1)
                dve.tensor_tensor(d.rhs[tc], w[tc], ps[tc, 6, 0:256].rearrange("p (j t) -> p j t", j=2),
                                  ALU.subtract).then_inc(delta_rhs_ready, 1)
                dve.wait_ge(delta_state, h_count + c)
                own(dve.tensor_tensor(state_p[:, hs], state[:, hs], decay(2 * n + c).broadcast_to([P, 2, P]), ALU.mult))
                dve.wait_ge(delta_u_summed, C + 1)
                dve.tensor_copy(d.u[tc].rearrange("p a b -> p (a b)"), ps[tc, 7, 0:256]).then_inc(delta_u_ready, 1)
                dve.wait_ge(delta_s_summed, C + 1)
                for hp in range(2):
                    r = slice(HD * hp, HD * hp + HD)
                    last = dve.tensor_tensor(state[r, hs, r], state_p[r, hs, r], ps[r, 0, 0:256].rearrange("p (j t) -> p j t", j=2)[:, :, r],
                                             ALU.add)
                last.then_inc(delta_state, 1)

        def mix_act(act, l):
            v = l + 1
            act.wait_ge(dve_evac, start_of["mix_in", (l, 0)])
            norm_act(act, 3 * l + 1, mod[:, 3 * KD:4 * KD])
            p0 = start_of["mix_in", (l, 0)]

            def piece(i, odd):
                s = (p0 + odd) % 2
                split_act(act, *ahead(p0, MIX_TILES // 2, WIDE, i, odd))
                act.wait_ge(piece_done, p0 + i + 1)
                act.activation(proj[:, bass.ds(2 * i, 1), :].rearrange("p a t -> p (a t)"), main[s][0], ACT.Copy).then_inc(act_evac, 1)
            steps(act, MIX_TILES // 2, piece)
            p_end = p0 + MIX_TILES // 2
            act.wait_ge(dve_evac, p_end)
            act.wait_ge(act_evac, p_end)
            act.activation(att_r[:], proj[:, 0:5], ACT.Square).then_inc(qk_squared, 1)
            act.wait_ge(qk_sums, v)
            act.activation(att_r[:, 0:4], ps[:, 4:8], ACT.Sqrt, bias=eps[:], scale=1.0 / HD)
            act.activation(att_r[:, 4], ps[:, 0], ACT.Sqrt, bias=eps[:], scale=1.0 / HD).then_inc(qk_roots, 1)

            def exps(u):
                U, g = 8 * l + u, u % 2
                wide = P if u < 2 else 2 * P
                act.wait_ge(att_max, U + 1)
                for j in range(4):
                    act.activation(att_s[:, g, j, 0:wide], att_s[:, g, j, 0:wide], ACT.Exp, bias=att_nm[:, g, j:j + 1],
                                   accum_out=att_den[:, g, j:j + 1])
                act.activation(att_es[:, g], att_dd[:, g], ACT.Exp).then_inc(att_exp, 1)
            exps(0)
            for u in range(8):
                n, g, U = u // 2, u % 2, 8 * l + u
                nk = 1 if n == 0 else 2
                if u < 7:
                    exps(u + 1)
                act.wait_ge(att_turned, U + 1)
                if U:
                    act.wait_ge(att_pv, U)
                act.activation(att_p[:, 0:nk], ps[:, 0:nk], ACT.Copy).then_inc(att_p_ready, 1)
                act.wait_ge(att_pv, U + 1)
                rows = slice(HD * g, HD * g + HD)
                act.activation(hn_hi[rows, 0:4, n * P:(n + 1) * P], ps[rows, 2 + g].rearrange("p (j t) -> p j t", j=4),
                               ACT.Copy).then_inc(att_out_hi, 1)
            act.wait_ge(shifted, v)
            act.activation(proj[0:HD, 12], proj[0:HD, 12], ACT.Tanh)
            act.activation(proj[:, 13], proj[:, 13], ACT.Sigmoid).then_inc(lora_ready, 1)
            act.wait_ge(lora_out, v)
            for j in range(2):
                act.activation(rw_sw[:, j], ps[:, 4 + j], ACT.Sigmoid, bias=vcol(l, "w0", j))
                act.activation(rw_a[:, j], ps[:, 6 + j], ACT.Sigmoid, bias=vcol(l, "a0", j))
            act.activation(rw_g[:], ps[:, 0:2], ACT.Copy).then_inc(gates_ready, 1)
            act.wait_ge(kk_raw, v)
            act.activation(rw_bonus[:], rw_kk[:], ACT.Square).then_inc(kk_squared, 1)
            act.wait_ge(kk_sums, v)
            act.activation(rw_r[:], ps[:, 4:6], ACT.Sqrt).then_inc(kk_norms, 1)
            act.wait_ge(logs_ready, v)
            act.activation(rw_kr[:, 1], rw_ls[:], ACT.Exp, scale=-DECAY_RATE)
            act.activation(rw_kr[:, 0], rw_sw[:], ACT.Exp, scale=-DECAY_RATE)
            act.activation(rw_ki[:], rw_ls[:], ACT.Exp, scale=DECAY_RATE)
            act.activation(rw_ed[:], rw_ed[:], ACT.Exp, scale=-DECAY_RATE).then_inc(decays_ready, 1)
            act.wait_ge(conv_ready, v)
            act.activation(hn_hi[:, 6:8], conv_y[:], ACT.Copy).then_inc(conv_hi, 1)
            act.wait_ge(rw_turned, v)
            act.activation(rw_vt[:].rearrange("p a b c -> p a (b c)"), ps[:, 4:6], ACT.Copy)
            act.activation(rw_bt[:].rearrange("p a b c -> p a (b c)"), ps[:, 6:8], ACT.Copy).then_inc(rw_tokens_a, 1)
            for n in range(NB):
                delta_act(act, rwu, l * NB + n, n, rw_y[:, :, n * P:(n + 1) * P], True)
            act.wait_ge(gn_centred, v)
            act.activation(rw_r[:], rw_y[:], ACT.Square).then_inc(gn_squared, 1)
            act.wait_ge(gn_square_sums, v)
            act.activation(rw_r[:], ps[:, 6:8], ACT.Sqrt, bias=gn_eps[:], scale=1.0 / HD).then_inc(gn_roots, 1)
            act.wait_ge(rw_out, v)
            act.activation(hn_hi[:, 4:6], rw_y[:], ACT.Copy).then_inc(rw_out_hi, 1)
            p1 = start_of["mix_out", (l, 0)]

            def out_piece(i, odd):
                s = (p1 + odd) % 2
                split_act(act, *ahead(p1, KD // 2, WIDE, i, odd))
                act.wait_ge(piece_done, p1 + i + 1)
                if isinstance(i, int) and i < 2:
                    act.wait_ge(mixed_ready, v)
                else:
                    act.wait_ge(dve_evac, p1 + i - 1)
                act.activation(tmp[:, s], main[s][0], ACT.Copy).then_inc(act_evac, 1)
            steps(act, KD // 2, out_piece)

        def mix_dve(dve, own, l):
            v = l + 1
            norm_dve(dve, own, 3 * l + 1, gains[:, l, 1], mod[:, 4 * KD:5 * KD], mod[:, 3 * KD:4 * KD])
            own(dve.tensor_scalar(out_gain[:], mod[:, 5 * KD:6 * KD], 1.0, None, ALU.add))
            p0 = start_of["mix_in", (l, 0)]

            def piece(i, odd):
                s = (p0 + odd) % 2
                split_dve(dve, *ahead(p0, MIX_TILES // 2, WIDE, i, odd))
                dve.wait_ge(piece_done, p0 + i + 1)
                dve.tensor_copy(proj[:, bass.ds(2 * i + 1, 1), :].rearrange("p a t -> p (a t)"), main[s][1]).then_inc(dve_evac, 1)
            steps(dve, MIX_TILES // 2, piece)
            if l == 0:
                dve.wait_ge(vec_loaded, 32)
                dve.wait_ge(masks_ready, 1)
            dve.wait_ge(qk_roots, v)
            own(dve.reciprocal(att_r[:], att_r[:]))
            dve.scalar_tensor_tensor(proj[:, 0:4], proj[:, 0:4], vcol(l, "q_gain"), att_r[:, 0:4], ALU.mult, ALU.mult)
            dve.scalar_tensor_tensor(proj[:, 4], proj[:, 4], vcol(l, "k_gain"), att_r[:, 4], ALU.mult, ALU.mult).then_inc(qk_normed, 1)
            dve.wait_ge(att_v_turned, v)
            dve.tensor_copy(att_v[:].rearrange("p a b -> p (a b)"), ps[:, 4]).then_inc(att_v_ready, 1)

            def masked(u):
                U, g = 8 * l + u, u % 2
                wide = P if u < 2 else 2 * P
                dve.wait_ge(att_scored, U + 1)
                if U >= 2:
                    dve.wait_ge(att_turned, U - 1)
                s = att_s[:, g, :, 0:wide]
                scores = ps[:, 4 + 2 * g:6 + 2 * g].rearrange("p b (j k) -> p (b j) k", k=256)[:, :, 0:wide]
                dve.scalar_tensor_tensor(s, scores, HD ** -0.5, band[:, 2 * P - wide:].unsqueeze(1).broadcast_to([P, 4, wide]),
                                         ALU.mult, ALU.add).then_inc(att_masked, 1)
                dve.wait_ge(att_masked, U + 1)
                own(dve.tensor_reduce(att_mx[:, g], s, AX.X, ALU.max))
                sk = sinks[:, l, 4 * g:4 * g + 4]
                own(dve.tensor_tensor(att_mx[:, g], att_mx[:, g], sk, ALU.max))
                own(dve.tensor_scalar(att_nm[:, g], att_mx[:, g], -1.0, None, ALU.mult))
                dve.tensor_tensor(att_dd[:, g], sk, att_nm[:, g], ALU.add).then_inc(att_max, 1)
            masked(0)
            for u in range(8):
                n, g, U = u // 2, u % 2, 8 * l + u
                wide = P if u < 2 else 2 * P
                if u < 7:
                    masked(u + 1)
                dve.wait_ge(att_exp, U + 1)
                own(dve.tensor_tensor(att_den[:, g], att_den[:, g], att_es[:, g], ALU.add))
                own(dve.reciprocal(att_den[:, g], att_den[:, g]))
                s = att_s[:, g, :, 0:wide]
                dve.tensor_tensor(s, s, att_den[:, g].unsqueeze(2).broadcast_to([P, 4, wide]), ALU.mult).then_inc(att_probs, 1)
                dve.wait_ge(att_out_hi, U + 1)
                rows = slice(HD * g, HD * g + HD)
                dve.tensor_tensor(hn_lo[rows, 0:4, n * P:(n + 1) * P], ps[rows, 2 + g].rearrange("p (j t) -> p j t", j=4),
                                  hn_hi[rows, 0:4, n * P:(n + 1) * P].bitcast(F32), ALU.subtract).then_inc(att_out, 1)

            r, k, val = proj[:, 6:8], proj[:, 8:10], proj[:, 10:12]
            dve.wait_ge(shifted, v)
            dve.wait_ge(att_pv, 8 * v)
            for j in range(2):
                last = dve.tensor_scalar(rw_kk[:, j], k[:, j], vcol(l, "k_k", j), None, ALU.mult)
            last.then_inc(kk_raw, 1)
            dve.wait_ge(gates_ready, v)
            for j in range(2):
                own(dve.tensor_tensor_scan(rw_ls[:, j], restart[:], rw_sw[:, j], 0.0, ALU.mult, ALU.add))
            own(dve.tensor_tensor(rw_sw[:], rw_ls[:], rw_sw[:], ALU.subtract))
            ls = rw_ls[:].rearrange("p j (c i) -> p (j c) i", i=HD)
            dve.wait_ge(conv_ready, v)
            dve.tensor_tensor(rw_ed[:].rearrange("p j (c i) -> p (j c) i", i=HD), ls[:, :, HD - 1:HD].broadcast_to([P, 16, HD]), ls,
                              ALU.subtract).then_inc(logs_ready, 1)
            dve.wait_ge(kk_norms, v)
            own(dve.tensor_scalar(rw_r[:], rw_r[:], 1e-12, None, ALU.max))
            own(dve.reciprocal(rw_r[:], rw_r[:]))
            own(dve.tensor_tensor(rw_kk[:], rw_kk[:], rw_r[:], ALU.mult))
            for j in range(2):
                own(dve.tensor_scalar(rw_r[:, j], rw_a[:, j], 1.0, vcol(l, "k_a", j), ALU.subtract, ALU.mult))
            own(dve.scalar_tensor_tensor(k, rw_r[:], 1.0, k, ALU.add, ALU.mult))
            own(dve.tensor_tensor(rw_a[:], rw_a[:], rw_kk[:], ALU.mult))
            own(dve.tensor_tensor(rw_bonus[:], r, k, ALU.mult))
            for j in range(2):
                last = dve.tensor_scalar(rw_bonus[:, j], rw_bonus[:, j], vcol(l, "r_k", j), None, ALU.mult)
            last.then_inc(bonus_raw, 1)
            dve.wait_ge(decays_ready, v)
            own(dve.tensor_copy(chunk_decay[:], rw_kr[:, 1].rearrange("p j (c i) -> p j c i", i=HD)[:, :, :, HD - 1]))
            dve.tensor_tensor(rw_kr[:, 0], rw_kr[:, 0], rw_kk[:], ALU.mult)
            dve.tensor_tensor(rw_kr[:, 1], rw_kr[:, 1], r, ALU.mult)
            dve.tensor_tensor(rw_bi[:], rw_a[:], rw_ki[:], ALU.mult)
            own(dve.tensor_tensor(rw_ki[:], k, rw_ki[:], ALU.mult))
            dve.tensor_tensor(rw_a[:], rw_a[:], rw_ed[:], ALU.mult)
            own(dve.tensor_tensor(rw_ed[:], k, rw_ed[:], ALU.mult))
            dve.wait_ge(bonus_sums, v)
            dve.tensor_tensor(rw_bonus[:], ps[:, 6:8], val, ALU.mult).then_inc(factors_ready, 1)
            dve.wait_ge(conv_hi, v)
            dve.tensor_tensor(hn_lo[:, 6:8], conv_y[:], hn_hi[:, 6:8].bitcast(F32), ALU.subtract)
            dve.wait_ge(rw_turned, v)
            dve.tensor_copy(rw_kt[:].rearrange("p a b c -> p a (b c)"), ps[:, 0:2]).then_inc(rw_tokens_b, 1)

            def mask_products():
                for hp in range(2):
                    low = ps[:, 4 + hp, 0:256].rearrange("p (j t) -> p j t", j=2)
                    dve.tensor_tensor(rwu.x[:, hp], low, pair_low[:].unsqueeze(1).broadcast_to([P, 2, P]), ALU.mult)
                    both = up_mask[:].unsqueeze(1).broadcast_to([P, 2, 2, P])
                    dve.tensor_tensor(rwu.mc[:, hp], ps[:, hp].rearrange("p (j w t) -> p j w t", j=2, w=2), both, ALU.mult)
                    last = dve.tensor_tensor(rwu.mb[:, hp], ps[:, 6 + hp].rearrange("p (j w t) -> p j w t", j=2, w=2), both, ALU.mult)
                own(last)
            for n in range(NB):
                if n == 0:
                    dve.wait_ge(shifted, v)
                    dve.wait_ge(rw_tokens_a, v)
                    own(dve.memset(state_p[:], 0.0))
                    dve.memset(state[:], 0.0).then_inc(delta_state, 1)
                delta_dve(dve, own, rwu, l * NB + n, n, 9 * l + 1 + 2 * n, lambda c: chunk_decay[:, :, c:c + 1], mask_products)
            dve.wait_ge(gn_sums, v)
            dve.scalar_tensor_tensor(rw_y[:], ps[:, 4:6], -1.0 / HD, rw_y[:], ALU.mult, ALU.add).then_inc(gn_centred, 1)
            dve.wait_ge(gn_roots, v)
            own(dve.reciprocal(rw_r[:], rw_r[:]))
            own(dve.tensor_tensor(rw_y[:], rw_y[:], rw_r[:], ALU.mult))
            for j in range(2):
                own(dve.tensor_scalar(rw_y[:, j], rw_y[:, j], vcol(l, "gn_w", j), vcol(l, "gn_b", j), ALU.mult, ALU.add))
            own(dve.tensor_tensor(rw_y[:], rw_y[:], rw_bonus[:], ALU.add))
            dve.tensor_tensor(rw_y[:], rw_y[:], rw_g[:], ALU.mult).then_inc(rw_out, 1)
            dve.wait_ge(rw_out, v)
            dve.wait_ge(rw_out_hi, v)
            dve.tensor_tensor(hn_lo[:, 4:6], rw_y[:], hn_hi[:, 4:6].bitcast(F32), ALU.subtract).then_inc(mixed_ready, 1)
            p1 = start_of["mix_out", (l, 0)]

            def out_piece(i, odd):
                s = (p1 + odd) % 2
                split_dve(dve, *ahead(p1, KD // 2, WIDE, i, odd))
                dve.wait_ge(act_evac, p1 + i + 1)
                for t in range(2):
                    hj = h[:, bass.ds(2 * i + t, 1), :].rearrange("p a t -> p (a t)")
                    src = tmp[:, s] if t == 0 else main[s][1]
                    last = dve.scalar_tensor_tensor(hj, src, out_gain[:, bass.ds(2 * i + t, 1)], hj, ALU.mult, ALU.add)
                last.then_inc(dve_evac, 1)
            steps(dve, KD // 2, out_piece)

        @block.tensor
        def _(pe):
            if LAYERS:
                pe_flush(pe, 0)
            for l in range(LAYERS):
                ffn_pe(pe, 2 * l)
                mix_pe(pe, l)
                ffn_pe(pe, 2 * l + 1)
            second_pe(pe)

        @block.scalar
        def _(act):
            act.wait_ge(small_loaded, 48)
            act.activation(csig[:], cvec[:], ACT.Sigmoid).then_inc(c_ready, 1)
            act.wait_ge(x_loaded, 16)
            act.wait_ge(const_ready, 2)
            split_act(act, (0, 0), WIDE)
            for l in range(LAYERS):
                act.wait_ge(dve_evac, start_of["up", (2 * l, 0)])
                ffn_act(act, 2 * l)
                mix_act(act, l)
                act.wait_ge(dve_evac, start_of["up", (2 * l + 1, 0)])
                ffn_act(act, 2 * l + 1)
            second_act(act)

        @block.vector
        def _(dve):
            own = Chain(dve, dve_own)
            dve.wait_ge(c_ready, 1)
            dve.tensor_tensor(cvec[:], cvec[:], csig[:], ALU.mult).then_inc(c_ready, 1)
            if LAYERS:
                dve_flush(dve, own, 0)
            split_dve(dve, (0, 0), WIDE)
            for l in range(LAYERS):
                ffn_dve(dve, own, 2 * l)
                mix_dve(dve, own, l)
                ffn_dve(dve, own, 2 * l + 1)
            second_dve(dve, own)


def mix_columns():
    import numpy as np
    heads = [h for j in range(4) for h in (j, j + 4)]
    q = [HD * h + i for h in heads for i in range(HD)]
    return np.array(q + list(range(len(q), MIX_TILES * P)))


def mix_rows():
    import numpy as np
    heads = [h for j in range(4) for h in (j, j + 4)]
    q = [HD * h + i for h in heads for i in range(HD)]
    return np.array(q + list(range(len(q), D)))


def host_vec(g):
    import numpy as np
    col = lambda v, n: v.reshape(DEPTH, n, P).transpose(2, 0, 1)
    parts = {
        "mu": col(g["rwkv_mu"], 8), "w0": col(g["rwkv_w0"], 2), "a0": col(g["rwkv_a0"], 2),
        "k_k": col(g["rwkv_k_k"], 2), "k_a": col(g["rwkv_k_a"], 2), "r_k": col(g["rwkv_r_k"], 2),
        "gn_w": col(g["rwkv_gn_w"], 2), "gn_b": col(g["rwkv_gn_b"], 2), "conv": col(g["conv_w"], 6),
        "q_gain": np.concatenate([g["att_q_gain"].T] * 2)[:, :, None],
        "k_gain": np.concatenate([g["att_k_gain"].T] * 2)[:, :, None],
    }
    return np.concatenate([parts[k] for k in VEC], 2)


def host_lora(g):
    import numpy as np
    wa = np.concatenate([g["rwkv_w_w2"], g["rwkv_a_w2"]], 1)
    return np.stack([wa, g["rwkv_g_w2"]], 1).transpose(2, 0, 1, 3)


def host_vec2(g):
    import numpy as np
    col = lambda v, n: v.reshape(n, P).T
    heads = np.zeros((2, P), np.float32)
    heads[0, 32:40], heads[1, 32:40] = g["a_log_2"][0], g["dt_bias_2"][0]
    return np.concatenate([col(g["norm_w_2"], 8), col(g["final_norm_w_2"], 8), col(g["conv_w_2"], 48),
                           np.concatenate([g["gdn_norm_w_2"].T] * 2), heads.T], 1)


def rope_tables():
    import numpy as np
    f32 = np.float32
    inv = (f32(10000.0) ** (-np.arange(0, HD, 2, dtype=f32) / f32(HD))).astype(f32)
    ang = np.arange(T, dtype=f32)[None, :] * np.tile(inv, 4)[:, None]
    both = np.stack([np.cos(ang), np.sin(ang)], 1).astype(f32)
    return np.stack([both.reshape(P, 2, T // d, d).transpose(0, 1, 3, 2).reshape(P, 2, T) for d in DILATION], 1)


def host_second(g):
    import numpy as np
    w = g["w_in_2"][0]
    ends = np.cumsum([0, 9 * 512, 512, 3 * 512, 512, 8, 8, D, D])
    dsa, dsa_z, gdn, gdn_z, b, a, gate_a, gate_b = [w[:, x:y] for x, y in zip(ends, ends[1:])]

    def pairs(m):
        k, n = m.shape
        return m.reshape(k // P, P, n // (2 * P), 2, P).transpose(2, 1, 0, 3, 4).reshape(n // (2 * P), P, k * 2)

    def single(m):
        k, n = m.shape
        return m.reshape(k // P, P, n // P, P).transpose(2, 1, 0, 3)

    ba = np.zeros((D, P), np.float32)
    ba[:, 0:8], ba[:, 32:40] = b, a
    merge = [np.concatenate([single(gate), single(up)], 2).reshape(KD, P, MERGE)
             for gate, up in ((gate_a, g["w_up_a_2"][0]), (gate_b, g["w_up_b_2"][0]))]
    return {
        "gdn_in": pairs(gdn)[None], "gdn_ba": single(ba).reshape(1, 1, P, D), "gdn_z": pairs(gdn_z)[None],
        "dsa_in": pairs(dsa).reshape(3, 6, P, WIDE), "dsa_z": pairs(dsa_z)[None],
        "merge": np.stack(merge), "last": pairs(g["w_out_2"][0])[None],
    }


def kernel(**inputs):
    import numpy as np
    import concourse.bacc as _bacc
    from concourse.bass_utils import run_bass_kernel_spmd as _run
    g = {k: np.asarray(v) for k, v in inputs.items()}
    nc = _bacc.Bacc("TRN2", target_bir_lowering=False, num_devices=1)
    tall = lambda v, n: v.reshape(*v.shape[:-1], n, P)
    def up(wt):
        return wt.reshape(DEPTH, KD, P, 2, NF, P).transpose(0, 4, 2, 1, 3, 5)
    def down(wt):
        return wt.reshape(DEPTH, 2, HALF, P, KD, P).transpose(0, 1, 4, 3, 2, 5)
    data = {
        "x": g["x"][0].T.reshape(KD, P, T).transpose(1, 0, 2),
        "c": g["c"][0].reshape(KD, P).T,
        "b_ada": g["b_ada"].reshape(DEPTH, NMOD * KD, P).transpose(2, 0, 1),
        "gains": np.stack([g["g_ffn1"], g["g_mix"], g["g_ffn2"]], 1).reshape(DEPTH, 3, KD, P).transpose(3, 0, 1, 2),
        "vec": host_vec(g),
        "lora": host_lora(g),
        "sinks": g["att_sinks"].reshape(1, DEPTH, 8),
        "vec2": host_vec2(g),
        "rope": rope_tables(),
        "mix_in": (g["w_mix_in"][:, :, mix_columns()].reshape(DEPTH, KD, P, MIX_TILES // 2, 2, P)
                   .transpose(0, 3, 2, 1, 4, 5).reshape(DEPTH, MIX_TILES // 2, P, WIDE)),
        "mix_out": (g["w_mix_out"][:, mix_rows()].reshape(DEPTH, KD, P, KD // 2, 2, P)
                    .transpose(0, 3, 2, 1, 4, 5).reshape(DEPTH, KD // 2, P, WIDE)),
        "ada": g["w_ada"].reshape(DEPTH, KD, P, ADA_PIECES, ADA_COLS).transpose(0, 3, 2, 1, 4),
        "up": np.stack([up(g["w_ffn1_in"]), up(g["w_ffn2_in"])], 1).reshape(2 * DEPTH, NF, P, WIDE),
        "down": np.stack([down(g["w_ffn1_out"]), down(g["w_ffn2_out"])], 1).reshape(2 * DEPTH, 2, KD, P, TALL),
    }
    data.update(host_second(g))
    arrays, aps = {}, {}
    for name, a in data.items():
        arrays["in_" + name] = np.ascontiguousarray(a)
        aps[name] = nc.dram_tensor("in_" + name, arrays["in_" + name].shape, F32, kind="ExternalInput").ap()
    ap_up, ap_down = aps["up"], aps["down"]
    aps["up"] = lambda at, i: ap_up[at[0], bass.ds(i + HALF * at[1], 1)].rearrange("a p n -> (a p) n")
    ap_mi, ap_mo = aps["mix_in"], aps["mix_out"]
    aps["mix_in"] = lambda at, i: ap_mi[at[0], bass.ds(i, 1)].rearrange("a p n -> (a p) n")
    aps["mix_out"] = lambda at, i: ap_mo[at[0], bass.ds(i, 1)].rearrange("a p n -> (a p) n")
    aps["down"] = lambda at, i: ap_down[at[0], at[1], bass.ds(i, 1)].rearrange("a p n -> (a p) n")
    for name in ("gdn_in", "gdn_ba", "gdn_z", "dsa_in", "dsa_z", "merge", "last"):
        def piece(at, i, ap=aps[name]):
            return ap[at, bass.ds(i, 1)].rearrange("a p n -> (a p) n")
        aps[name] = piece
    out = nc.dram_tensor("out", (P, KD, T), F32, kind="ExternalOutput").ap()
    program(nc, aps, out)
    r = _run(nc, [arrays], core_ids=[0])
    return np.ascontiguousarray(r.results[0]["out"].transpose(2, 1, 0).reshape(1, T, D))
```
